# Optimizing a Trainium2 kernel written in Bass

```python
import math
import jax, jax.numpy as jnp
from jax import lax
import numpy as np

D_MODEL = 1024
BATCH = 1
SEQ = 256
DEPTH = 2

GRID_W = 64
CTX_LEN = 256
HEAD_DIM = 64
A_HEADS = 8
A_KV_HEADS = 2
ROPE_THETA = 10000.0
Q_BLOCK = 128
B_HEADS = 4
WIN_ROWS_MAX = 8
WIN_COLS = 16
C_CH = 256
C_SHORT = 3
C_POS_BANDS = 16
C_POS_DIM = 2 * C_POS_BANDS + 1
C_FILTER_HIDDEN = 64
C_DECAY_TARGET = 1e-2
C_FAST_DECAY = 0.3
C_SLOW_DECAY = 1.5
A_W = A_HEADS * HEAD_DIM
A_KV_W = A_KV_HEADS * HEAD_DIM
B_W = B_HEADS * HEAD_DIM
MIX_W = A_W + B_W + C_CH
A_Q0 = 0
A_K0 = A_Q0 + A_W
A_V0 = A_K0 + A_KV_W
B_Q0 = A_V0 + A_KV_W
B_K0 = B_Q0 + B_W
B_V0 = B_K0 + B_W
C0 = B_V0 + B_W
PROJ_W = C0 + 3 * C_CH
N_EXPERTS = 64
TOP_K = 8
N_GROUPS = 8
TOPK_GROUPS = 4
EXPERT_HIDDEN = 128
SHARED_HIDDEN = 256
ROUTED_SCALE = 2.5
DN_ALPHA = (2 * DEPTH) ** 0.25
DN_BETA = (8 * DEPTH) ** -0.25
LN_EPS = 1e-6
RMS_EPS = 1e-6

kernel_name = "hybrid_dit_gqa_natten_hyena_moe"

F32 = jnp.float32

def layer_norm(x, g=None, b=None):
    xf = x.astype(F32)
    mu = jnp.mean(xf, -1, keepdims=True)
    var = jnp.mean(jnp.square(xf - mu), -1, keepdims=True)
    y = (xf - mu) * lax.rsqrt(var + LN_EPS)
    if g is not None:
        y = y * g.astype(F32) + b.astype(F32)
    return y.astype(x.dtype)

def rms_norm(x, g):
    xf = x.astype(F32)
    y = xf * lax.rsqrt(jnp.mean(jnp.square(xf), -1, keepdims=True) + RMS_EPS) * g.astype(F32)
    return y.astype(x.dtype)

def ada_modulation(cvec, w, b):
    m = jax.nn.silu(cvec) @ w + b
    return jnp.split(m, 6, axis=-1)

def modulate(x, shift, scale):
    return layer_norm(x) * (1 + scale) + shift

def to_heads(t, n):
    return t.reshape(t.shape[:-1] + (n, HEAD_DIM))

def axial_rope(n_tok):
    t = jnp.arange(n_tok)
    row = (t // GRID_W).astype(F32)
    col = (t % GRID_W).astype(F32)
    half = HEAD_DIM // 2
    inv = ROPE_THETA ** (-jnp.arange(0, half, 2, dtype=F32) / half)
    ang = jnp.concatenate([row[:, None] * inv, col[:, None] * inv], -1)
    return jnp.cos(ang), jnp.sin(ang)

def apply_rope(x, cos, sin):
    xf = x.astype(F32)
    x1, x2 = xf[..., 0::2], xf[..., 1::2]
    out = jnp.stack([x1 * cos - x2 * sin, x1 * sin + x2 * cos], -1).reshape(x.shape)
    return out.astype(x.dtype)

def dense_attention(q, k, v):
    bsz, lq, h, dh = q.shape
    g = k.shape[2]
    qg = q.reshape(bsz, lq, g, h // g, dh)
    s = jnp.einsum('bqgrd,bkgd->bgrqk', qg, k).astype(F32) * (dh ** -0.5)
    p = jax.nn.softmax(s, -1).astype(v.dtype)
    o = jnp.einsum('bgrqk,bkgd->bqgrd', p, v)
    return o.reshape(bsz, lq, h * dh)

def gqa_latent(q, k, v, k_ctx, v_ctx):
    bsz, n = q.shape[:2]
    nb = n // Q_BLOCK
    rep = A_HEADS // A_KV_HEADS
    kk = jnp.concatenate([k_ctx, k], 1)
    vv = jnp.concatenate([v_ctx, v], 1)
    qb = q.reshape(bsz, nb, Q_BLOCK, A_KV_HEADS, rep, HEAD_DIM).transpose(1, 0, 3, 4, 2, 5)
    scale = HEAD_DIM ** -0.5

    def block(qi):
        s = jnp.einsum('bgrqd,bkgd->bgrqk', qi, kk).astype(F32) * scale
        p = jax.nn.softmax(s, -1).astype(vv.dtype)
        return jnp.einsum('bgrqk,bkgd->bgrqd', p, vv)

    o = lax.map(block, qb)
    return o.transpose(1, 0, 4, 2, 3, 5).reshape(bsz, n, A_W)

def neighbourhood_attention(q, k, v, k_ctx, v_ctx, rpb):
    bsz, n = q.shape[:2]
    rows = n // GRID_W
    wr = min(WIN_ROWS_MAX, rows)
    grid = lambda t: t.reshape(bsz, rows, GRID_W, B_HEADS, HEAD_DIM)
    qg, kg, vg = grid(q), grid(k), grid(v)
    col = np.arange(GRID_W)
    col_start = np.clip(col - WIN_COLS // 2, 0, GRID_W - WIN_COLS)
    col_idx = col_start[:, None] + np.arange(WIN_COLS)[None, :]
    dc = col_idx - col[:, None] + WIN_COLS - 1
    scale = HEAD_DIM ** -0.5
    n_win = wr * WIN_COLS

    def row_block(r):
        rs = jnp.clip(r - wr // 2, 0, rows - wr)
        qr = lax.dynamic_index_in_dim(qg, r, axis=1, keepdims=False)
        kr = lax.dynamic_slice_in_dim(kg, rs, wr, axis=1)
        vr = lax.dynamic_slice_in_dim(vg, rs, wr, axis=1)
        kw = kr[:, :, col_idx]
        vw = vr[:, :, col_idx]
        dr = rs + jnp.arange(wr) - r + WIN_ROWS_MAX - 1
        bias = rpb[:, dr[None, :, None], dc[:, None, :]].astype(F32)
        s_win = jnp.einsum('bqhd,biqjhd->bhqij', qr, kw).astype(F32) * scale + bias[None]
        s_ctx = jnp.einsum('bqhd,bkhd->bhqk', qr, k_ctx).astype(F32) * scale
        s = jnp.concatenate([s_win.reshape(bsz, B_HEADS, GRID_W, n_win), s_ctx], -1)
        p = jax.nn.softmax(s, -1).astype(v.dtype)
        p_win = p[..., :n_win].reshape(bsz, B_HEADS, GRID_W, wr, WIN_COLS)
        p_ctx = p[..., n_win:]
        return (jnp.einsum('bhqij,biqjhd->bqhd', p_win, vw)
                + jnp.einsum('bhqk,bkhd->bqhd', p_ctx, v_ctx))

    o = lax.map(row_block, jnp.arange(rows))
    return o.transpose(1, 0, 2, 3, 4).reshape(bsz, n, B_W)

def short_conv(z, w, b):
    n = z.shape[1]
    p = C_SHORT // 2
    zp = jnp.pad(z, ((0, 0), (p, C_SHORT - 1 - p), (0, 0)))
    return sum(zp[:, i:i + n] * w[i] for i in range(C_SHORT)) + b

def implicit_filters(n, w1, b1, w2, b2, w3, freq):
    t = jnp.linspace(0.0, 1.0, n, dtype=F32)[:, None]
    w = 2 * math.pi * jnp.arange(n, dtype=F32)[:, None] / n
    f = jnp.linspace(1e-4, C_POS_BANDS - 1, C_POS_BANDS, dtype=F32)[None]
    z = jnp.concatenate([t, jnp.cos(f * w), -jnp.sin(f * w)], -1)
    h = jnp.sin(freq[0].astype(F32) * (z @ w1.astype(F32) + b1.astype(F32)))
    h = jnp.sin(freq[1].astype(F32) * (h @ w2.astype(F32) + b2.astype(F32)))
    h = h @ w3.astype(F32)
    lo = math.log(C_DECAY_TARGET) / C_SLOW_DECAY
    hi = math.log(C_DECAY_TARGET) / C_FAST_DECAY
    deltas = jnp.abs(jnp.linspace(lo, hi, C_CH, dtype=F32))
    decay = jnp.exp(-t * deltas[None])
    return h[:, :C_CH] * decay, h[:, C_CH:] * decay

def bidir_long_conv(u, hf, hb):
    n = u.shape[1]
    k = jnp.concatenate([hf, jnp.zeros((1, C_CH), F32), hb[1:][::-1]], 0)
    kf = jnp.fft.rfft(k, n=2 * n, axis=0)
    uf = jnp.fft.rfft(u.astype(F32), n=2 * n, axis=1)
    y = jnp.fft.irfft(uf * kf[None], n=2 * n, axis=1)[:, :n]
    return y.astype(u.dtype)

def hyena_mixer(z, conv_w, conv_b, f_w1, f_b1, f_w2, f_b2, f_w3, freq, skip):
    n = z.shape[1]
    z = short_conv(z, conv_w, conv_b)
    x0, x1, v = jnp.split(z, 3, axis=-1)
    hf, hb = implicit_filters(n, f_w1, f_b1, f_w2, f_b2, f_w3, freq)
    u = v * x1
    y = bidir_long_conv(u, hf, hb) + u * skip
    return y * x0

def moe_ffn(h, rw, rb, w1, w3, w2, sw1, sw3, sw2):
    t = h.shape[0]
    scores = jax.nn.sigmoid((h @ rw).astype(F32))
    sel = scores + rb.astype(F32)
    grp = sel.reshape(t, N_GROUPS, N_EXPERTS // N_GROUPS)
    gscore = lax.top_k(grp, 2)[0].sum(-1)
    _, gidx = lax.top_k(gscore, TOPK_GROUPS)
    gmask = jax.nn.one_hot(gidx, N_GROUPS, dtype=F32).sum(1) > 0
    emask = jnp.repeat(gmask, N_EXPERTS // N_GROUPS, axis=1)
    _, eidx = lax.top_k(jnp.where(emask, sel, -jnp.inf), TOP_K)
    wsel = jnp.take_along_axis(scores, eidx, -1)
    wsel = wsel / jnp.sum(wsel, -1, keepdims=True) * ROUTED_SCALE
    gate = jnp.sum(jax.nn.one_hot(eidx, N_EXPERTS, dtype=F32) * wsel[..., None], 1)
    a = jnp.einsum('td,edh->teh', h, w1)
    b = jnp.einsum('td,edh->teh', h, w3)
    act = (jax.nn.silu(a) * b * gate[..., None].astype(h.dtype))
    routed = jnp.einsum('teh,ehd->td', act, w2)
    shared = (jax.nn.silu(h @ sw1) * (h @ sw3)) @ sw2
    return (routed + shared).astype(h.dtype)

def moe_per_sample(h, rw, rb, w1, w3, w2, sw1, sw3, sw2):
    return lax.map(lambda hs: moe_ffn(hs, rw, rb, w1, w3, w2, sw1, sw3, sw2), h)

def setup_inputs(seed: int = 0) -> dict:
    key = jax.random.key(seed)
    ks = iter(jax.random.split(key, 40))
    nrm = lambda shape, s: jax.random.normal(next(ks), shape, F32) * s
    D = D_MODEL
    L = DEPTH
    return {
        "x": nrm((BATCH, SEQ, D), 1.0),
        "c": nrm((BATCH, D), 1.0),
        "ctx": nrm((BATCH, CTX_LEN, D), 1.0),
        "c_ctx": nrm((D,), 1.0),
        "ada_w": nrm((L, D, 6 * D), 0.5 * D ** -0.5),
        "ada_b": nrm((L, 6 * D), 0.02),
        "w_in": nrm((L, D, PROJ_W), D ** -0.5),
        "q_gain": 1.0 + nrm((L, HEAD_DIM), 0.05),
        "k_gain": 1.0 + nrm((L, HEAD_DIM), 0.05),
        "nat_rpb": nrm((L, B_HEADS, 2 * WIN_ROWS_MAX - 1, 2 * WIN_COLS - 1), 0.1),
        "hy_conv_w": nrm((L, C_SHORT, 3 * C_CH), 0.5),
        "hy_conv_b": nrm((L, 3 * C_CH), 0.02),
        "hy_f_w1": nrm((L, C_POS_DIM, C_FILTER_HIDDEN), C_POS_DIM ** -0.5),
        "hy_f_b1": nrm((L, C_FILTER_HIDDEN), 0.1),
        "hy_f_w2": nrm((L, C_FILTER_HIDDEN, C_FILTER_HIDDEN), C_FILTER_HIDDEN ** -0.5),
        "hy_f_b2": nrm((L, C_FILTER_HIDDEN), 0.1),
        "hy_f_w3": nrm((L, C_FILTER_HIDDEN, 2 * C_CH), 0.01),
        "hy_freq": 1.0 + nrm((L, 2, C_FILTER_HIDDEN), 0.1),
        "hy_skip": nrm((L, C_CH), 0.5),
        "w_out": nrm((L, MIX_W, D), DN_BETA * MIX_W ** -0.5),
        "ln1_g": 1.0 + nrm((L, D), 0.05),
        "ln1_b": nrm((L, D), 0.02),
        "router_w": nrm((L, D, N_EXPERTS), D ** -0.5),
        "router_b": nrm((L, N_EXPERTS), 0.01),
        "exp_w1": nrm((L, N_EXPERTS, D, EXPERT_HIDDEN), D ** -0.5),
        "exp_w3": nrm((L, N_EXPERTS, D, EXPERT_HIDDEN), D ** -0.5),
        "exp_w2": nrm((L, N_EXPERTS, EXPERT_HIDDEN, D), DN_BETA * EXPERT_HIDDEN ** -0.5),
        "sh_w1": nrm((L, D, SHARED_HIDDEN), D ** -0.5),
        "sh_w3": nrm((L, D, SHARED_HIDDEN), D ** -0.5),
        "sh_w2": nrm((L, SHARED_HIDDEN, D), DN_BETA * SHARED_HIDDEN ** -0.5),
        "ln2_g": 1.0 + nrm((L, D), 0.05),
        "ln2_b": nrm((L, D), 0.02),
    }

def reference(x, c, ctx, c_ctx, ada_w, ada_b, w_in, q_gain, k_gain, nat_rpb, hy_conv_w, hy_conv_b,
              hy_f_w1, hy_f_b1, hy_f_w2, hy_f_b2, hy_f_w3, hy_freq, hy_skip, w_out, ln1_g, ln1_b,
              router_w, router_b, exp_w1, exp_w3, exp_w2, sh_w1, sh_w3, sh_w2, ln2_g, ln2_b):
    n_lat = x.shape[1]
    cos, sin = axial_rope(n_lat)
    cos, sin = cos[:, None, :], sin[:, None, :]
    xc = ctx
    for l in range(DEPTH):
        last = l == DEPTH - 1
        sh1, sc1, g1, sh2, sc2, g2 = [m[:, None, :] for m in ada_modulation(c, ada_w[l], ada_b[l])]
        csh1, csc1, cg1, csh2, csc2, cg2 = ada_modulation(c_ctx, ada_w[l], ada_b[l])
        w = w_in[l]
        hy_args = (hy_conv_w[l], hy_conv_b[l], hy_f_w1[l], hy_f_b1[l], hy_f_w2[l], hy_f_b2[l],
                   hy_f_w3[l], hy_freq[l], hy_skip[l])
        moe_args = (router_w[l], router_b[l], exp_w1[l], exp_w3[l], exp_w2[l],
                    sh_w1[l], sh_w3[l], sh_w2[l])

        hc = modulate(xc, csh1, csc1)
        if last:
            pkv_a = hc @ w[:, A_K0:B_Q0]
            pkv_b = hc @ w[:, B_K0:C0]
        else:
            pc = hc @ w
            pkv_a = pc[..., A_K0:B_Q0]
            pkv_b = pc[..., B_K0:C0]
        kca = rms_norm(to_heads(pkv_a[..., :A_KV_W], A_KV_HEADS), k_gain[l])
        vca = to_heads(pkv_a[..., A_KV_W:], A_KV_HEADS)
        kcb = to_heads(pkv_b[..., :B_W], B_HEADS)
        vcb = to_heads(pkv_b[..., B_W:], B_HEADS)
        if not last:
            qca = rms_norm(to_heads(pc[..., A_Q0:A_K0], A_HEADS), q_gain[l])
            qcb = to_heads(pc[..., B_Q0:B_K0], B_HEADS)
            oc = jnp.concatenate([dense_attention(qca, kca, vca),
                                  dense_attention(qcb, kcb, vcb),
                                  hyena_mixer(pc[..., C0:], *hy_args)], -1)
            xc_mid = layer_norm(DN_ALPHA * xc + cg1 * (oc @ w_out[l]), ln1_g[l], ln1_b[l])
            hc2 = modulate(xc_mid, csh2, csc2)
            xc = layer_norm(DN_ALPHA * xc_mid + cg2 * moe_per_sample(hc2, *moe_args), ln2_g[l], ln2_b[l])

        hx = modulate(x, sh1, sc1)
        px = hx @ w
        qa = apply_rope(rms_norm(to_heads(px[..., A_Q0:A_K0], A_HEADS), q_gain[l]), cos, sin)
        ka = apply_rope(rms_norm(to_heads(px[..., A_K0:A_V0], A_KV_HEADS), k_gain[l]), cos, sin)
        va = to_heads(px[..., A_V0:B_Q0], A_KV_HEADS)
        qb = to_heads(px[..., B_Q0:B_K0], B_HEADS)
        kb = to_heads(px[..., B_K0:B_V0], B_HEADS)
        vb = to_heads(px[..., B_V0:C0], B_HEADS)
        ox = jnp.concatenate([gqa_latent(qa, ka, va, kca, vca),
                              neighbourhood_attention(qb, kb, vb, kcb, vcb, nat_rpb[l]),
                              hyena_mixer(px[..., C0:], *hy_args)], -1)
        x = layer_norm(DN_ALPHA * x + g1 * (ox @ w_out[l]), ln1_g[l], ln1_b[l])
        hx2 = modulate(x, sh2, sc2)
        x = layer_norm(DN_ALPHA * x + g2 * moe_per_sample(hx2, *moe_args), ln2_g[l], ln2_b[l])
    return x


_drawn_inputs = setup_inputs


def setup_inputs(seed=0):
    import zlib

    import numpy as np

    out = dict(_drawn_inputs(seed))
    spreads = {}
    factors = {'ctx': 4.282,
     'q_gain': 8.0,
     'k_gain': 8.0,
     'nat_rpb': 53.084,
     'hy_conv_b': 8.0,
     'hy_f_w1': 2.695,
     'hy_f_b1': 8.0,
     'hy_f_w2': 2.814,
     'hy_f_b2': 8.0,
     'hy_f_w3': 2.865,
     'hy_freq': 8.0}
    for name, (base, spread) in spreads.items():
        noise = np.random.default_rng([zlib.crc32(name.encode()), seed]).standard_normal(out[name].shape)
        drawn = base * np.exp(spread * noise) if base else spread * noise
        out[name] = __import__('jax').numpy.asarray(drawn.astype(out[name].dtype))
    for name, factor in factors.items():
        out[name] = (out[name] * factor).astype(out[name].dtype)
    return out
```

```python
import math
from contextlib import ExitStack

import concourse.bass as bass
import numpy as np
from concourse import mybir

F32 = mybir.dt.float32
BF16 = mybir.dt.bfloat16
F16 = mybir.dt.float16
I32 = mybir.dt.int32
U32 = mybir.dt.uint32
ALU = mybir.AluOpType
ACT = mybir.ActivationFunctionType
AX = mybir.AxisListType

P = 128
DEPTH = 2
D = 1024
KD = D // P
SEQ = 256
GRID_W = 64
HEAD = 64
A_HEADS, A_KV, B_HEADS = 8, 2, 4
A_W, A_KV_W, B_W, C_CH = 512, 128, 256, 256
A_K0 = A_W
B_Q0 = A_K0 + 2 * A_KV_W
B_V0 = B_Q0 + 2 * B_W
C0 = B_V0 + B_W
MIX = A_W + B_W + C_CH
EXPERTS, TOP_K, GROUPS, TOP_GROUPS, HIDDEN, SHARED = 64, 8, 8, 4, 128, 256
ROUTED_SCALE = 2.5
ALPHA = (2 * DEPTH) ** 0.25
EPS = 1e-6
BANDS = 16
POS = 2 * BANDS + 1
FHID = 64
HALF = 512
TILES = 4
STREAMS = ((0, 1), (2, 3))
FULL = ((0, 1, 2, 3), (2, 3))
SLOTS = 128
UNROLL = 4
RING = 3
MASKED = -1e30
ROTATING = 6


def turns_of(l):
    tokens = P * len(FULL[l])
    worst = EXPERTS + (tokens * TOP_K - EXPERTS) // SLOTS
    return EXPERTS // UNROLL, -(-worst // UNROLL)


BLOCKS_MAX = UNROLL * max(turns_of(l)[1] for l in range(DEPTH)) + 1

CONST = {}
_at = 0
for _n, _w in (("ident", P), ("cos", 2 * 32), ("sin", 2 * 32), ("iota_slot", SLOTS), ("iota_block", BLOCKS_MAX),
               ("before8", 64), ("token", TILES)):
    CONST[_n] = (_at, _at + _w)
    _at += _w
CONST_W = _at
ONCE = {}
_at = 0
for _n, _w in (("before128", P), ("ones", P), ("start64", EXPERTS), ("upto64", EXPERTS)):
    ONCE[_n] = (_at, _at + _w)
    _at += _w
ONCE_W = _at


def constants():
    t = np.arange(SEQ)
    half = HEAD // 2
    inv = (10000.0 ** (-np.arange(0, half, 2, dtype=np.float32) / half)).astype(np.float32)
    ang = np.concatenate([(t // GRID_W).astype(np.float32)[:, None] * inv,
                          (t % GRID_W).astype(np.float32)[:, None] * inv], -1).astype(np.float32)
    tab = np.zeros((P, CONST_W), np.float32)

    def put(a, table, name, v):
        a[:, table[name][0]:table[name][1]] = v

    put(tab, CONST, "ident", np.eye(P))
    put(tab, CONST, "cos", np.cos(ang).reshape(2, P, 32).transpose(1, 0, 2).reshape(P, 64))
    put(tab, CONST, "sin", np.sin(ang).reshape(2, P, 32).transpose(1, 0, 2).reshape(P, 64))
    put(tab, CONST, "iota_slot", np.arange(SLOTS))
    put(tab, CONST, "iota_block", np.arange(BLOCKS_MAX))
    g = np.arange(GROUPS)
    put(tab, CONST, "before8", (g[None, :] < g[:, None]).reshape(1, 64))
    put(tab, CONST, "token", np.arange(P)[:, None] + P * np.arange(TILES))
    once = np.zeros((P, ONCE_W), np.float32)
    i = np.arange(P)
    e = np.arange(EXPERTS)
    put(once, ONCE, "before128", i[:, None] < i[None, :])
    put(once, ONCE, "ones", 1.0)
    once[:EXPERTS, ONCE["start64"][0]:ONCE["start64"][1]] = SLOTS * (e[:, None] < e[None, :])
    once[:EXPERTS, ONCE["upto64"][0]:ONCE["upto64"][1]] = e[:, None] <= e[None, :]
    theta = 2 * np.pi * (np.arange(SEQ) + 0.5) / (2 * SEQ)
    c, s = np.cos(np.outer(t, theta)), np.sin(np.outer(t, theta))
    fwd = np.stack([c.reshape(2, P, SEQ), s.reshape(2, P, SEQ)], 1)
    inv_ = np.stack([c.T.reshape(2, P, SEQ), s.T.reshape(2, P, SEQ)], 1) / SEQ
    dft = np.stack([fwd, inv_]).transpose(3, 0, 1, 2, 4).reshape(P, 8 * SEQ).astype(np.float32)
    col = t % GRID_W
    first = np.clip(col - 8, 0, GRID_W - 16)
    inside = (col[None, :] >= first[:, None]) & (col[None, :] < first[:, None] + 16)
    mask = np.where(inside, 0.0, MASKED).astype(np.float32).reshape(2, P, SEQ).transpose(1, 0, 2)
    tt = np.linspace(0.0, 1.0, SEQ, dtype=np.float32)[:, None]
    w = (2 * math.pi * np.arange(SEQ, dtype=np.float32)[:, None] / SEQ).astype(np.float32)
    f = np.linspace(1e-4, BANDS - 1, BANDS, dtype=np.float32)[None]
    z = np.concatenate([tt, np.cos(f * w), -np.sin(f * w)], -1).astype(np.float32).T
    lo, hi = math.log(1e-2) / 1.5, math.log(1e-2) / 0.3
    deltas = np.abs(np.linspace(lo, hi, C_CH, dtype=np.float32))
    decay = np.exp(-tt * deltas[None]).astype(np.float32)
    back = decay.copy()
    back[0] = 0.0
    both = np.stack([decay, back], 1).reshape(2, P, 2 * C_CH).transpose(1, 0, 2)
    return {"tab": tab, "once": once, "dft": dft, "mask": np.ascontiguousarray(mask),
            "pos": np.ascontiguousarray(z), "decay": np.ascontiguousarray(both)}


class Banks:

    def __init__(self):
        self.order, self.of, self.read = [], {}, {"scalar": 0, "vector": 0}

    def add(self, name, reader):
        self.read[reader] += 1
        self.of[name] = (len(self.order), reader, self.read[reader])
        self.order.append(name)

    def filled(self, name):
        return self.of[name][0] + 1

    def before(self, name):
        j = self.of[name][0] - ROTATING
        return self.of[self.order[j]][1:] if j >= 0 else None


def attention_units():
    units = []
    for l in range(DEPTH):
        mine = []
        for t in FULL[l]:
            keys = (0, 1) if t < 2 else (0, 1, 2, 3)
            mine += [(t, "A", h, keys) for h in (0, 4, 1, 5, 2, 6, 3, 7)]
            mine += [(t, "B", h, keys) for h in range(B_HEADS)]
        units.append(mine)
    return units


S_AHEAD, PV_LAG = 2, 1


def plan():
    jobs, units = Banks(), attention_units()
    for l in range(DEPTH):
        for m in (0, 1):
            jobs.add(("fil1", l), "vector") if m == 0 else jobs.add(("fil2", l), "vector")
        for tt in (0, 1):
            jobs.add(("fil3", l, tt), "vector")
        for m in (0, 1):
            for cs in (0, 1):
                jobs.add(("filK", l, m, cs), "vector")
    for l in range(DEPTH):
        full = FULL[l]
        for c in range(4):
            jobs.add(("ada", l, c), "scalar")
        for t in range(TILES):
            for h in (0, 1):
                jobs.add(("hT", l, 1, t, h), ("scalar", "vector")[h])
        for t in full:
            jobs.add(("q", l, t), "scalar")
        for t in range(TILES):
            jobs.add(("kv", l, t), "scalar")
        for f in range(4):
            jobs.add(("bqk", l, f), "scalar")
        for f in range(6):
            jobs.add(("c", l, f), "scalar")
        for c in range(4, 12):
            jobs.add(("ada", l, c), "scalar")
        for t in range(TILES):
            if t in full:
                jobs.add(("qT", l, t), "scalar")
            jobs.add(("kT", l, t), "scalar")
        for t in full:
            jobs.add(("uT", l, t), "scalar")
        for m in (0, 1):
            for cs in (0, 1):
                jobs.add(("U", l, m, cs), "vector")
        for ct in (0, 1):
            jobs.add(("yh", l, ct), "vector")
        n = len(units[l])
        for i in range(n + S_AHEAD + PV_LAG):
            if i < n:
                jobs.add(("S", l, i), "scalar")
            if 0 <= i - S_AHEAD < n:
                u = i - S_AHEAD
                jobs.add(("PT", l, u), ("vector", "scalar")[u % 2])
        for t in full:
            for h in (0, 1):
                jobs.add(("oT", l, t, h), "scalar")
        for t in full:
            for h in (0, 1):
                jobs.add(("wo", l, t, h), "vector")
        for t in full:
            for h in (0, 1):
                jobs.add(("hT", l, 2, t, h), ("scalar", "vector")[h])
        jobs.add(("rt", l), "scalar")
        for t in full[:-1]:
            jobs.add(("sh", l, t), "vector")
        jobs.add(("count", l), "vector")
        jobs.add(("ends", l), "vector")
        jobs.add(("list", l), "vector")
        jobs.add(("pos", l), "vector")
        jobs.add(("idx", l), "vector")
        jobs.add(("sh", l, full[-1]), "vector")
        for t in full:
            jobs.add(("sT", l, t), "scalar")
            for h in (0, 1):
                jobs.add(("sy", l, t, h), "scalar")
    return jobs, units


def last_job(it):
    kind, l = it[0], it[1]
    return {"dft": ("filK", DEPTH - 1, 1, 1), "ada": it, "mixc": ("yh", l, 1), "wo": ("wo", l, TILES - 1, 1),
            "sw13": ("sh", l, TILES - 1), "sw2": ("sy", l, TILES - 1, 1),
            "win": (("q", l, TILES - 1), ("kv", l, TILES - 1), ("bqk", l, 3), ("c", l, 3), ("c", l, 5))[it[-1] if kind == "win" else 0]}[kind]


def weight_items():
    items = [("dft", 0)]
    for l in range(DEPTH):
        items += [("ada", l, c) for c in range(4)]
        items += [("win", l, b) for b in range(5)]
        items += [("ada", l, c) for c in range(4, 12)]
        items += [("mixc", l), ("wo", l, 0), ("wo", l, 1), ("sw13", l), ("sw2", l)]
    return items


def hybrid_backbone(nc, a, out, scratch):
    jobs, units = plan()
    items = weight_items()
    item_at = {it: n for n, it in enumerate(items)}
    unit_base = (0, len(units[0]))
    with ExitStack() as ctx:
        def sb(name, cols, dt=F32, rows=P):
            return ctx.enter_context(nc.sbuf_tensor(name, [rows, cols], dt))

        def sem(name):
            return ctx.enter_context(nc.semaphore(name))

        X = sb("residual", TILES * D)[:, :].rearrange("p (t d) -> p t d", t=TILES)
        HN = sb("tokens_h", TILES * D)[:, :].rearrange("p (t d) -> p t d", t=TILES)
        HT = sb("features_h", KD * HALF)[:, :].rearrange("p (k t) -> p k t", k=KD)
        QKV = sb("qkv", TILES * D)[:, :].rearrange("p (t d) -> p t d", t=TILES)
        BQK_ = sb("b_qk", 4 * HALF)
        CP_ = sb("c_padded", 6 * 2 * (SEQ + 2))
        QA_ = sb("a_q", 4 * HALF)
        KA = sb("a_k", HALF)
        MODA = sb("shift_scale", 4 * D)[:, :].rearrange("p (w v d) -> p w v d", w=2, v=2)
        MODG = sb("gate_rows", 2 * D)[:, :].rearrange("p (v d) -> p v d", v=2)
        LNB = sb("norm_rows", 2 * D)[:, :].rearrange("p (w d) -> p w d", w=2)
        WB = sb("weights", RING * 4096)
        KF = sb("filters", DEPTH * 4 * C_CH)[:, :].rearrange("p (l m s c) -> p l m s c", l=DEPTH, m=2, s=2)
        TAB = sb("tab", CONST_W)
        GAIN = sb("gains", DEPTH * 2 * HEAD)[:, :].rearrange("p (l w d) -> p l w d", l=DEPTH, w=2)
        HYC = sb("hyena_columns", DEPTH * 26)[:, :].rearrange("p (l c) -> p l c", l=DEPTH)
        MROW = sb("mod_rows", 2 * HALF, rows=2)[:, :].rearrange("p (s c) -> p s c", s=2)
        RW = sb("router_w", KD * EXPERTS)[:, :].rearrange("p (k e) -> p k e", k=KD)
        RB = sb("router_b", DEPTH * EXPERTS)[:, :].rearrange("p (l e) -> p l e", l=DEPTH)
        PB = sb("probs", 2 * HALF)[:, :].rearrange("p (s c) -> p s c", s=2)
        PT = sb("probs_T", 2 * HALF)[:, :].rearrange("p (s c) -> p s c", s=2)
        ONE_S = sb("onehot_slot", 4 * SLOTS, F16)[:, :].rearrange("p (s c) -> p s c", s=4)
        ONE_B = sb("onehot_block", 4 * BLOCKS_MAX, F16)[:, :].rearrange("p (s c) -> p s c", s=4)
        TRI = sb("count_tables", ONCE_W, BF16)
        SIL = sb("silu_a", HIDDEN)
        ACTV = sb("expert_act", HIDDEN)
        ACTT = sb("expert_act_T", SLOTS)
        CS = sb("silu_c", KD * 2)[:, :].rearrange("p (k v) -> p k v", k=KD)
        STAT = sb("stats", TILES * 12)[:, :].rearrange("p (t c) -> p t c", t=TILES)
        MV = sb("mean_var", TILES * 2)[:, :].rearrange("p (t c) -> p t c", t=TILES)
        RS = sb("rstd", 40, I32)
        NV = sb("newton_v", 40)
        NT = sb("newton_t", 40)
        SS = sb("square_sums", 40)
        NM = sb("neg_max", 4)
        SM = sb("prob_sum", 4)
        RC = sb("prob_recip", 4)
        POSI = sb("row_of_choice", TILES * 8, I32)[:, :].rearrange("p (t j) -> p t j", t=TILES)
        P8 = sb("choice_keys", TILES * 8)[:, :].rearrange("p (t j) -> p t j", t=TILES)
        G8 = sb("choice_gates", TILES * 8)[:, :].rearrange("p (t j) -> p t j", t=TILES)
        PSB = sb("slot_and_block", 4 * TILES * 8, I32)[:, :].rearrange("p (w c) -> p w c", w=4)
        IDX = sb("token_of_slot", BLOCKS_MAX, I32)
        IDXB = sb("gather_index", 2, I32)
        LIST = sb("block_experts", BLOCKS_MAX + 1, I32, rows=1)
        NB1 = sb("block_counts", 8)

        BQK = BQK_[:, :].rearrange("p (f t) -> p f t", f=4)
        CP = CP_[:, :].rearrange("p (f s t) -> p f s t", f=6, s=2)
        QA = QA_[:, :].rearrange("p (c t) -> p c t", c=4)
        OT = HT
        QN = HN[:, 0:3, :].rearrange("p t d -> p (t d)")[:, 0:4 * 640].rearrange("p (t h d) -> p t h d", t=4, h=10)
        MASK_SB = HN[:, 2, 512:1024].rearrange("p (t c) -> p t c", t=2)
        SQ = HN[:, 3, 0:640].rearrange("p (h d) -> p h d", h=10)
        RP = PB.rearrange("p s c -> p (s c)")[:, 0:640].rearrange("p (w h d) -> p w h d", w=2, h=10)
        OTOK = HN
        MACC = QKV
        UT = CP_[:, 0:4 * C_CH].rearrange("p (t c) -> p t c", t=4)
        YF = CP_[:, 4 * C_CH:4 * C_CH + 4 * HALF].rearrange("p (m s c) -> p m s c", m=2, s=2)
        XG = QA_[:, :].rearrange("p (s d) -> p s d", s=2)
        XGT = BQK_[:, :].rearrange("p (s k t) -> p s k t", s=2, k=KD)
        YSB = HN
        RT = CP_[:, 0:12 * 256].rearrange("p (a c) -> p a c", a=12)
        SG = PB.rearrange("p s c -> p (s c)")[:, 0:2 * SHARED].rearrange("p (s c) -> p s c", s=2)
        SA = PB.rearrange("p s c -> p (s c)")[:, 2 * SHARED:4 * SHARED].rearrange("p (s c) -> p s c", s=2)
        SAW = QKV
        ST = PT.rearrange("p s c -> p (s c)")[:, 0:4 * P].rearrange("p (s h t) -> p s h t", s=2, h=2)
        YG = [QA_[:, 0:D], QA_[:, D:2 * D], BQK_[:, 0:D], BQK_[:, D:2 * D]]
        ONCE_SB = QKV[:, 0, 0:ONCE_W]
        POS_SB = QKV[0:POS, 1, 0:SEQ]
        FW1 = QKV[0:POS, 1, SEQ:SEQ + DEPTH * FHID].rearrange("p (l c) -> p l c", l=DEPTH)
        FW2 = QKV[0:FHID, 1, 384:384 + DEPTH * FHID].rearrange("p (l c) -> p l c", l=DEPTH)
        FCOL = QKV[0:FHID, 1, 512:512 + DEPTH * 4].rearrange("p (l c) -> p l c", l=DEPTH)
        FW3 = QKV[0:FHID, 2, :].rearrange("p (l c) -> p l c", l=DEPTH)
        DECAY = QKV[:, 3, :].rearrange("p (t c) -> p t c", t=2)
        FH = HT[:, 0:4, 0:SEQ]
        FT = HT[:, 4:6, :]
        FS = HT[:, 6:8, :]

        def const(name):
            return TAB[:, CONST[name][0]:CONST[name][1]]

        def table(name, rows=P):
            return TRI[0:rows, ONCE[name][0]:ONCE[name][1]]

        ident = const("ident")

        def ring(n):
            return WB[:, (n % RING) * 4096:(n % RING + 1) * 4096]

        def item(it):
            return ring(item_at[it])

        def expert_w(u):
            r = WB[:, u * 3072:(u + 1) * 3072]
            return r[:, 0:2048].rearrange("p (m k h) -> p m k h", m=2, k=KD), r[:, 2048:3072]

        PS = [ctx.enter_context(nc.psum_tensor(f"bank{i}", [P, HALF], F32)) for i in range(8)]
        O_BANK = PS[6:8]
        XT_PS, AB_PS, AT_PS, Y_PS = PS[0:2], PS[2], PS[3], PS[4:6]

        def bank(name):
            return PS[jobs.of[name][0] % ROTATING]

        consts_in = sem("consts_in")
        once_in = sem("once_in")
        x_in = sem("x_in")
        ring_in = [sem(f"ring_in{i}") for i in range(RING)]
        bias_used = sem("window_bias_used")
        mask_in = sem("mask_in")
        small_in = sem("small_rows_in")
        router_in = sem("router_in")
        bank_filled = sem("bank_filled")
        by_scalar = sem("read_by_scalar")
        by_vector = sem("read_by_vector")
        vector_step = sem("vector_step")
        silu_c = sem("silu_c_ready")
        sin_arg = sem("sin_arg_ready")
        sin_out = sem("sin_ready")
        filt_ready = sem("filter_sums_ready")
        tables_ready = sem("tables_ready")
        row_sent = [sem(f"mod_row_sent{i}") for i in range(2)]
        bias_rows = sem("mod_bias_in_dram")
        moda_in = sem("shift_scale_in")
        modg_in = sem("gate_rows_in")
        norm_in = sem("norm_rows_in")
        moda_used = sem("shift_scale_used")
        modg_used = sem("gate_rows_used")
        norm_used = sem("norm_rows_used")
        h_ready = sem("h_ready")
        h_stored = sem("h_stored")
        qn_ready = sem("qk_normed")
        u_ready = sem("hyena_u_ready")
        yf_ready = sem("hyena_product_ready")
        pads_ready = sem("pads_ready")
        max_ready = sem("neg_max_ready")
        o_filled = sem("attention_product_done")
        o_read = sem("attention_output_ready")
        mask_ready = sem("choice_ready")
        nb_ready = sem("block_counts_ready")
        ends_ready = sem("block_ends_ready")
        onehot = sem("onehots_ready")
        onehot_used = sem("onehots_used")
        list_ready = sem("block_list_ready")
        sg_ready = sem("shared_silu_ready")
        sa_ready = sem("shared_act_ready")
        idx_ready = sem("token_list_ready")
        choices_ready = sem("choice_rows_ready")
        zeros_ready = sem("dummy_block_ready")
        gathered = [sem(f"choice_gathered{i}") for i in range(4)]
        choice_used = sem("choice_added")
        rows_filled = sem("spare_rows_filled")
        y_sent = sem("expert_rows_in_dram")
        out_ready = sem("output_ready")
        out_sent = sem("output_sent")
        loop = [{n: sem(f"{n}_{l}") for n in (
            "w_in0", "w_in1", "w_in2", "w_in3", "x_in0", "x_in1", "y_out0", "y_out1", "index_copied", "gathers",
            "xT_ps", "xT_scalar", "xT_vector", "ab_ps", "silu", "act", "actT_ps", "actT", "y_ps", "y_scalar",
            "y_vector")} for l in range(DEPTH)]

        h_dram, y_dram, mod_dram = scratch
        block = ctx.enter_context(nc.Block())

        @block.sync
        def _(sp):
            def load(dst, src, s, inc=16):
                sp.dma_start(dst, src).then_inc(s, inc)

            load(TAB[:, :], a["tab"], consts_in)
            load(CS, a["cond"], consts_in)
            load(HYC, a["hyc"], consts_in)
            load(ONCE_SB, a["once"], once_in)
            load(POS_SB, a["pos"], once_in)
            load(FW1, a["f_w1"], once_in)
            load(FW2, a["f_w2"], once_in)
            load(FCOL, a["f_col"], once_in)
            load(FW3, a["f_w3"], once_in)
            load(DECAY, a["decay"], once_in)

            def ring_load(n):
                it = items[n]
                if n >= RING:
                    sp.wait_ge(bank_filled, jobs.filled(last_job(items[n - RING])))
                if n >= RING and items[n - RING][0] == "mixc":
                    sp.wait_ge(bias_used, items[n - RING][1] + 1)
                s, kind, dst = ring_in[n % RING], it[0], ring(n)
                if kind == "dft":
                    load(dst[:, 0:4 * SEQ], a["dft"][:, 0:4 * SEQ], s, 32)
                elif kind == "ada":
                    load(dst.rearrange("p (k c) -> p k c", k=KD),
                         a["ada_w"][it[1]].rearrange("(p k) c -> p k c", k=KD)[:, :, it[2] * HALF:(it[2] + 1) * HALF],
                         s, 32)
                elif kind == "win":
                    w = a["w_in"][it[1]].rearrange("(p k) c -> p k c", k=KD)
                    d = dst.rearrange("p (k c) -> p k c", k=KD)
                    parts = {0: [(0, 0, 512)], 1: [(0, A_K0, 256), (256, B_V0, 256)], 2: [(0, B_Q0, 512)],
                             3: [(0, C0, 512)], 4: [(0, C0 + 512, 256)]}[it[2]]
                    for at, c, n_ in parts:
                        load(d[:, :, at:at + n_], w[:, :, c:c + n_], s, 32 // len(parts))
                elif kind == "mixc":
                    load(dst[:, 0:8 * SEQ], a["dft"], s)
                    load(dst[:, 8 * SEQ:16 * SEQ], a["rpb"][it[1]], s)
                elif kind == "wo":
                    w = a["w_out"][it[1]]
                    d = dst.rearrange("p (c n) -> p c n", c=KD)
                    cols = slice(it[2] * HALF, (it[2] + 1) * HALF)
                    for s_ in (0, 1):
                        load(d[64 * s_:64 * s_ + 64, 0:4, :],
                             w[256 * s_:256 * s_ + 256, cols].rearrange("(c d) n -> d c n", c=4), s, 16)
                    load(d[:, 4:8, :], w[512:1024, cols].rearrange("(c p) n -> p c n", p=P), s, 16)
                elif kind == "sw13":
                    d = dst.rearrange("p (m k c) -> p m k c", m=2, k=KD)
                    for m, name in ((0, "sh_w1"), (1, "sh_w3")):
                        load(d[:, m], a[name][it[1]].rearrange("(p k) c -> p k c", k=KD), s)
                elif kind == "sw2":
                    load(dst[:, 0:2 * D].rearrange("p (c n) -> p c n", c=2),
                         a["sh_w2"][it[1]].rearrange("(c p) n -> p c n", p=P), s, 32)

            at = 0
            for l in range(DEPTH):
                last = item_at[("sw2", l)]
                while at <= last:
                    if at == 3 and l == 0:
                        for t in range(TILES):
                            src = a["ctx"] if t < 2 else a["x"]
                            load(X[:, t, :], src[(t % 2) * P:(t % 2 + 1) * P, :], x_in)
                    ring_load(at)
                    at += 1
                    if items[at - 1] == ("wo", 0, 1):
                        sp.wait_ge(by_vector, jobs.of[("filK", DEPTH - 1, 1, 1)][2])
                        rest = BLOCKS_MAX - EXPERTS
                        load(y_dram[EXPERTS + 1:BLOCKS_MAX + 1].rearrange("b s d -> s b d"),
                             KF[:, 0].rearrange("p m s c -> p (m s c)").unsqueeze(1).to_broadcast([P, rest, D]), rows_filled)
                    if items[at - 1][0] == "mixc":
                        if l >= 1:
                            sp.wait_ge(bank_filled, jobs.filled(("rt", l - 1)))
                        load(RW, a["router_w"][l].rearrange("(p k) e -> p k e", k=KD), router_in)
                L = loop[l]
                sp.wait_ge(bank_filled, jobs.filled(last_job(("sw2", l))))
                sp.wait_ge(zeros_ready, l + 1)
                sp.wait_ge(list_ready, 2 * (l + 1))
                always, most = turns_of(l)
                blocks = sp.value_load(LIST[0:1, BLOCKS_MAX:BLOCKS_MAX + 1], min_val=EXPERTS, max_val=UNROLL * most)
                turns = sp.snap((blocks + UNROLL - 1) // UNROLL)

                def turn(i):
                    for u in range(UNROLL):
                        b = i * UNROLL + u
                        e = sp.value_load(LIST[0:1, bass.ds(b, 1)], min_val=0, max_val=EXPERTS - 1)
                        sp.wait_ge(L["y_ps"], b * 2 + 4)
                        w13, w2 = expert_w(u)
                        for m, name in ((0, "exp_w1"), (1, "exp_w3")):
                            load(w13[:, m], a[name][l][bass.ds(e, 1), :, :].rearrange("a (p k) h -> (a p) k h", k=KD),
                                 L[f"w_in{u}"])
                        load(w2, a["exp_w2"][l][bass.ds(e, 1), :, :].rearrange("a h d -> (a h) d"), L[f"w_in{u}"])

                with sp.Fori(0, always) as i:
                    turn(i)
                with sp.Fori(always, most) as i:
                    with sp.If(i < turns):
                        turn(i)
                sp.wait_ge(L["y_ps"], turns * (2 * UNROLL) + 10)
                sp.wait_ge(y_sent, l + 1)
            for t in FULL[-1]:
                sp.wait_ge(out_ready, t - 1)
                sp.dma_start(out[(t % 2) * P:(t % 2 + 1) * P, :], X[:, t, :]).then_inc(out_sent, 16)
            sp.wait_ge(out_sent, 16 * len(FULL[-1]))

        @block.tensor
        def _(pe):
            waited = {"scalar": by_scalar, "vector": by_vector}

            def start(name):
                was = jobs.before(name)
                if was:
                    pe.wait_ge(waited[was[0]], was[1])
                return bank(name)

            def read_out(name):
                _, who, n = jobs.of[name]
                pe.wait_ge(waited[who], n)

            def arrived(it):
                n = item_at[it]
                pe.wait_ge(ring_in[n % RING], sum(48 if x[0] == "wo" else 32 for x in items[n % RING:n + 1:RING]))
                return item(it)

            pe.wait_ge(once_in, 7 * 16)
            dft0 = arrived(("dft", 0))[:, 0:4 * SEQ].rearrange("p (t s m) -> p t s m", t=2, s=2)
            for l in range(DEPTH):
                b = start(("fil1", l))
                pe.matmul(b[0:FHID, 0:SEQ], FW1[:, l, :], POS_SB, start=True, stop=True).then_inc(bank_filled, 1)
                b = start(("fil2", l))
                pe.wait_ge(sin_out, 2 * l + 1)
                pe.matmul(b[0:FHID, 0:SEQ], FW2[:, l, :], FH[0:FHID, 2, :], start=True, stop=True).then_inc(bank_filled, 1)
                pe.wait_ge(sin_out, 2 * l + 2)
                for tt in (0, 1):
                    b = start(("fil3", l, tt))
                    pe.matmul(b[:, :], FH[0:FHID, 3, tt * P:(tt + 1) * P], FW3[:, l, :], start=True,
                              stop=True).then_inc(bank_filled, 1)
                pe.wait_ge(filt_ready, l + 1)
                for m in (0, 1):
                    for cs in (0, 1):
                        b = start(("filK", l, m, cs))
                        for tt in (0, 1):
                            mm = pe.matmul(b[:, 0:C_CH], dft0[:, tt, cs, m * P:(m + 1) * P],
                                           FS[:, tt, cs * C_CH:(cs + 1) * C_CH], start=tt == 0, stop=tt == 1)
                        mm.then_inc(bank_filled, 1)
            read_out(("filK", DEPTH - 1, 1, 1))

            def ada(l, c):
                w = arrived(("ada", l, c)).rearrange("p (k c) -> p k c", k=KD)
                b = start(("ada", l, c))
                for k in range(KD):
                    mm = pe.matmul(b[0:2, :], CS[:, k, :], w[:, k, :], start=k == 0, stop=k == KD - 1)
                mm.then_inc(bank_filled, 1)

            def transposed_h(l, which, t, n):
                pe.wait_ge(h_ready, n)
                for h in (0, 1):
                    b = start(("hT", l, which, t, h))
                    for k in range(4):
                        mm = pe.transpose(b[:, k * P:(k + 1) * P], HN[:, t, 4 * h + k:D:KD], ident)
                    mm.then_inc(bank_filled, 1)

            h_count = 0
            for l in range(DEPTH):
                full = FULL[l]
                if l == 0:
                    pe.wait_ge(silu_c, 1)
                for c in range(4):
                    ada(l, c)
                for t in range(TILES):
                    h_count += 1
                    transposed_h(l, 1, t, h_count)
                for h in (0, 1):
                    read_out(("hT", l, 1, TILES - 1, h))
                w = arrived(("win", l, 0)).rearrange("p (k c) -> p k c", k=KD)
                for t in full:
                    b = start(("q", l, t))
                    for k in range(KD):
                        mm = pe.matmul(b[:, :], HT[:, k, t * P:(t + 1) * P], w[:, k, :], start=k == 0, stop=k == KD - 1)
                    mm.then_inc(bank_filled, 1)
                w = arrived(("win", l, 1)).rearrange("p (k c) -> p k c", k=KD)
                for t in range(TILES):
                    b = start(("kv", l, t))
                    for k in range(KD):
                        mm = pe.matmul(b[:, :], HT[:, k, t * P:(t + 1) * P], w[:, k, :], start=k == 0, stop=k == KD - 1)
                    mm.then_inc(bank_filled, 1)
                first = full[0] * P
                w = arrived(("win", l, 2)).rearrange("p (k c) -> p k c", k=KD)
                for f in range(4):
                    lo = first if f < 2 else 0
                    b = start(("bqk", l, f))
                    for k in range(KD):
                        mm = pe.matmul(b[:, lo:HALF], w[:, k, f * P:(f + 1) * P], HT[:, k, lo:HALF],
                                       start=k == 0, stop=k == KD - 1)
                    mm.then_inc(bank_filled, 1)
                for f in range(6):
                    w = arrived(("win", l, 3 + f // 4)).rearrange("p (k c) -> p k c", k=KD)
                    b = start(("c", l, f))
                    for k in range(KD):
                        mm = pe.matmul(b[:, first:HALF], w[:, k, (f % 4) * P:(f % 4 + 1) * P], HT[:, k, first:HALF],
                                       start=k == 0, stop=k == KD - 1)
                    mm.then_inc(bank_filled, 1)
                for c in range(4, 12):
                    ada(l, c)
                for t in range(TILES):
                    pe.wait_ge(qn_ready, TILES * l + t + 1)
                    if t in full:
                        b = start(("qT", l, t))
                        for c in range(4):
                            mm = pe.transpose(b[:, c * P:(c + 1) * P], QN[:, t, 2 * c:2 * c + 2, :].rearrange("p h d -> p (h d)"), ident)
                        mm.then_inc(bank_filled, 1)
                    b = start(("kT", l, t))
                    pe.transpose(b[:, 0:P], QN[:, t, 8:10, :].rearrange("p h d -> p (h d)"), ident).then_inc(bank_filled, 1)
                pe.wait_ge(u_ready, l + 1)
                for t in full:
                    b = start(("uT", l, t))
                    for ct in (0, 1):
                        mm = pe.transpose(b[:, ct * P:(ct + 1) * P], OT[:, 2 + ct, t * P:(t + 1) * P], ident)
                    mm.then_inc(bank_filled, 1)
                read_out(("uT", l, full[-1]))
                mixc = arrived(("mixc", l))
                fwd = mixc[:, 0:4 * SEQ].rearrange("p (t s m) -> p t s m", t=2, s=2)
                inv = mixc[:, 4 * SEQ:8 * SEQ].rearrange("p (m s t) -> p m s t", m=2, s=2)
                ns = len(full) // 2
                uts = UT.rearrange("p (s t) c -> p t s c", t=2)
                for m in (0, 1):
                    for cs in (0, 1):
                        b = start(("U", l, m, cs))
                        for tt in (0, 1):
                            mm = pe.matmul(b[:, 0:ns * C_CH].rearrange("p (s c) -> p s c", s=ns),
                                           fwd[:, tt, cs, m * P:(m + 1) * P], uts[:, tt, 2 - ns:2, :],
                                           start=tt == 0, stop=tt == 1)
                        mm.then_inc(bank_filled, 1)
                pe.wait_ge(yf_ready, 2 * (l + 1))
                for ct in (0, 1):
                    b = start(("yh", l, ct))
                    for s in range(ns):
                        for m in (0, 1):
                            for cs in (0, 1):
                                mm = pe.matmul(b[:, s * SEQ:(s + 1) * SEQ],
                                               YF[:, m, cs, s * C_CH + ct * P:s * C_CH + (ct + 1) * P],
                                               inv[:, m, cs, :], start=m + cs == 0, stop=m + cs == 2)
                    mm.then_inc(bank_filled, 1)
                for t in range(TILES):
                    if t in full:
                        read_out(("qT", l, t))
                    read_out(("kT", l, t))

                mine = units[l]
                n = len(mine)

                def scores(u):
                    t, kind, h, keys = mine[u]
                    nk = len(keys) * P
                    b = start(("S", l, u))
                    if kind == "A":
                        lo = 64 * (h // 4)
                        q, k = QA[lo:lo + 64, h % 4, t * P:(t + 1) * P], KA[lo:lo + 64, 0:nk]
                    else:
                        lo = 64 * (h % 2)
                        q, k = BQK[lo:lo + 64, h // 2, t * P:(t + 1) * P], BQK[lo:lo + 64, 2 + h // 2, 0:nk]
                    pe.matmul(b[:, 0:nk], q, k, start=True, stop=True).then_inc(bank_filled, 1)

                def transposed(u):
                    keys = mine[u][3]
                    read_out(("S", l, u))
                    b = start(("PT", l, u))
                    for kt in keys:
                        mm = pe.transpose(b[:, kt * P:(kt + 1) * P], PB[:, u % 2, kt * P:(kt + 1) * P], ident)
                    mm.then_inc(bank_filled, 1)

                def product(u):
                    t, kind, h, keys = mine[u]
                    read_out(("PT", l, u))
                    U = unit_base[l] + u
                    if U >= 2:
                        pe.wait_ge(o_read, U - 1)
                    o = O_BANK[U % 2][:, 0:HEAD]
                    v0 = 640 + 64 * (h // 4) if kind == "A" else 768 + 64 * h
                    for kt in keys:
                        mm = pe.matmul(o, PT[:, u % 2, kt * P:(kt + 1) * P], QKV[:, kt, v0:v0 + 64],
                                       start=kt == keys[0], stop=kt == keys[-1])
                    mm.then_inc(o_filled, 1)

                for i in range(n + S_AHEAD + PV_LAG):
                    if i < n:
                        scores(i)
                    if 0 <= i - S_AHEAD < n:
                        transposed(i - S_AHEAD)
                    if 0 <= i - S_AHEAD - PV_LAG < n:
                        product(i - S_AHEAD - PV_LAG)
                pe.wait_ge(o_read, unit_base[l] + n)
                for t in full:
                    for h in (0, 1):
                        b = start(("oT", l, t, h))
                        for c in range(4 * h, 6 if h else 4):
                            mm = pe.transpose(b[:, (c % 4) * P:(c % 4 + 1) * P], OTOK[:, t, c * P:(c + 1) * P], ident)
                        mm.then_inc(bank_filled, 1)
                read_out(("oT", l, full[-1], 1))
                read_out(("yh", l, 1))
                pe.wait_ge(yf_ready, 2 * (l + 1))
                wo = [arrived(("wo", l, h)).rearrange("p (c n) -> p c n", c=KD) for h in (0, 1)]
                for t in full:
                    for h in (0, 1):
                        b = start(("wo", l, t, h))
                        for c in range(KD):
                            mm = pe.matmul(b[:, :], OT[:, c, t * P:(t + 1) * P], wo[h][:, c, :],
                                           start=c == 0, stop=c == KD - 1)
                        mm.then_inc(bank_filled, 1)

                for t in full:
                    h_count += 1
                    transposed_h(l, 2, t, h_count)
                for h in (0, 1):
                    read_out(("hT", l, 2, full[-1], h))
                pe.wait_ge(router_in, 16 * (l + 1))
                b = start(("rt", l))
                for g, t in enumerate(full):
                    for k in range(KD):
                        mm = pe.matmul(b[:, g * EXPERTS:(g + 1) * EXPERTS], HT[:, k, t * P:(t + 1) * P], RW[:, k, :],
                                       start=k == 0, stop=k == KD - 1)
                mm.then_inc(bank_filled, 1)
                sw13 = arrived(("sw13", l)).rearrange("p (m k c) -> p m k c", m=2, k=KD)

                def shared_in(t):
                    b = start(("sh", l, t))
                    for k in range(KD):
                        mm = pe.matmul(b[:, :].rearrange("p (m c) -> p m c", m=2), HT[:, k, t * P:(t + 1) * P],
                                       sw13[:, :, k, :], start=k == 0, stop=k == KD - 1)
                    mm.then_inc(bank_filled, 1)

                for t in full[:-1]:
                    shared_in(t)
                M16 = RT[:, 10, :].bitcast(BF16)
                NB16 = RT[:, 11, :].bitcast(BF16)
                pe.wait_ge(tables_ready, 1)
                pe.wait_ge(mask_ready, l + 1)
                b = start(("count", l))
                for g in range(len(full)):
                    mm = pe.matmul(b[0:EXPERTS, 0:1], M16[:, g * EXPERTS:(g + 1) * EXPERTS], table("ones")[:, 0:1],
                                   start=g == 0, stop=g == len(full) - 1)
                mm.then_inc(bank_filled, 1)
                pe.wait_ge(nb_ready, l + 1)
                b = start(("ends", l))
                pe.matmul(b[0:EXPERTS, 0:1], table("upto64", EXPERTS), NB16[0:EXPERTS, 0:1],
                          start=True, stop=True).then_inc(bank_filled, 1)
                pe.wait_ge(ends_ready, l + 1)
                b = start(("list", l))
                pe.matmul(b[0:1, 0:BLOCKS_MAX], table("ones", EXPERTS)[:, 0:1], NB16[0:EXPERTS, 256:256 + BLOCKS_MAX],
                          start=True, stop=True)
                pe.matmul(b[0:1, BLOCKS_MAX:BLOCKS_MAX + 1], NB16[0:EXPERTS, 0:1], table("ones", EXPERTS)[:, 0:1],
                          start=True, stop=True).then_inc(bank_filled, 1)
                b = start(("pos", l))
                for g in range(len(full)):
                    o = b[:, g * EXPERTS:(g + 1) * EXPERTS]
                    for g2 in range(g + 1):
                        pe.matmul(o, table("before128" if g2 == g else "ones"),
                                  M16[:, g2 * EXPERTS:(g2 + 1) * EXPERTS], start=g2 == 0, stop=False)
                    mm = pe.matmul(o, NB16[0:EXPERTS, 128:256], table("start64", EXPERTS), start=False, stop=True)
                mm.then_inc(bank_filled, 1)
                b = start(("idx", l))
                for n_ in range(len(full) * TOP_K):
                    N_ = n_ + l * TOP_K * len(FULL[0])
                    pe.wait_ge(onehot, N_ + 1)
                    pe.matmul(b[0:SLOTS, 0:BLOCKS_MAX], ONE_S[:, N_ % 4, :], ONE_B[:, N_ % 4, :],
                              start=n_ == 0, stop=n_ == len(full) * TOP_K - 1).then_inc(
                                  bank_filled if n_ == len(full) * TOP_K - 1 else onehot_used, 1)
                shared_in(full[-1])
                sw2 = arrived(("sw2", l))[:, 0:2 * D].rearrange("p (c n) -> p c n", c=2)
                for g, t in enumerate(full):
                    pe.wait_ge(sa_ready, len(FULL[0]) * l + g + 1)
                    b = start(("sT", l, t))
                    for c in (0, 1):
                        mm = pe.transpose(b[:, c * P:(c + 1) * P], SAW[:, t, c * P:(c + 1) * P], ident)
                    mm.then_inc(bank_filled, 1)
                    read_out(("sT", l, t))
                    for h in (0, 1):
                        b = start(("sy", l, t, h))
                        for c in (0, 1):
                            mm = pe.matmul(b[:, :], ST[:, g % 2, c, :], sw2[:, c, h * HALF:(h + 1) * HALF],
                                           start=c == 0, stop=c == 1)
                        mm.then_inc(bank_filled, 1)

                L = loop[l]
                read_out(("sy", l, full[-1], 1))
                read_out(("idx", l))
                pe.sem_inc(L["y_ps"], 8)
                pe.sem_inc(L["xT_ps"], 1)
                pe.wait_ge(zeros_ready, l + 1)
                pe.wait_ge(list_ready, 2 * (l + 1))
                always, most = turns_of(l)
                blocks = pe.value_load(LIST[0:1, BLOCKS_MAX:BLOCKS_MAX + 1], min_val=EXPERTS, max_val=UNROLL * most)
                turns = pe.snap((blocks + UNROLL - 1) // UNROLL)

                def tokens_T(v):
                    for k in range(KD):
                        mm = pe.transpose(XT_PS[k // 4][:, (k % 4) * SLOTS:(k % 4 + 1) * SLOTS],
                                          XG[0:SLOTS, v, k:D:KD], ident[0:SLOTS, 0:SLOTS])
                    mm.then_inc(L["xT_ps"], 1)

                def act_T():
                    pe.transpose(AT_PS[:, 0:SLOTS], ACTV[0:SLOTS, :], ident[0:SLOTS, 0:SLOTS]).then_inc(L["actT_ps"], 1)

                def second(u):
                    w2 = expert_w(u)[1]
                    for h in (0, 1):
                        pe.matmul(Y_PS[h][0:SLOTS, :], ACTT[:, :], w2[:, h * HALF:(h + 1) * HALF],
                                  start=True, stop=True).then_inc(L["y_ps"], 1)

                def turn(i):
                    for u in range(UNROLL):
                        b = i * UNROLL + u
                        pe.wait_ge(L["act"], b + 1)
                        act_T()
                        pe.wait_ge(L[f"x_in{(u + 1) % 2}"], i * 32 + 16 * ((u + 1) // 2 + 1))
                        pe.wait_ge(L["xT_scalar"], b + 1)
                        pe.wait_ge(L["xT_vector"], b + 1)
                        tokens_T((u + 1) % 2)
                        pe.wait_ge(L[f"w_in{u}"], i * 48 + 48)
                        w13 = expert_w(u)[0]
                        for k in range(KD):
                            mm = pe.matmul(AB_PS[0:SLOTS, 0:2 * HIDDEN].rearrange("p (m h) -> p m h", m=2),
                                           XGT[:, u % 2, k, :], w13[:, :, k, :], start=k == 0, stop=k == KD - 1)
                        mm.then_inc(L["ab_ps"], 1)
                        pe.wait_ge(L["actT"], b + 1)
                        pe.wait_ge(L["y_scalar"], b + 1)
                        pe.wait_ge(L["y_vector"], b + 1)
                        second((u - 1) % UNROLL)

                pe.wait_ge(L["x_in0"], 16)
                tokens_T(0)
                with pe.Fori(0, always) as i:
                    turn(i)
                with pe.Fori(always, most) as i:
                    with pe.If(i < turns):
                        turn(i)
                total = turns * UNROLL
                pe.wait_ge(L["act"], total + 1)
                pe.wait_ge(L["act"], EXPERTS)
                act_T()
                pe.wait_ge(L["actT"], total + 1)
                pe.wait_ge(L["y_scalar"], total + 1)
                pe.wait_ge(L["y_vector"], total + 1)
                pe.wait_ge(L["y_vector"], EXPERTS)
                second(UNROLL - 1)
                pe.wait_ge(L["xT_scalar"], total + 1)
                pe.wait_ge(L["xT_vector"], total + 1)
                pe.wait_ge(L["y_scalar"], total + 2)
                pe.wait_ge(L["y_vector"], total + 2)
                pe.wait_ge(L["y_vector"], EXPERTS)

        @block.scalar
        def _(act):
            done = [0]
            steps = [0]

            def filled(name):
                act.wait_ge(bank_filled, jobs.filled(name))
                return bank(name)

            def drained(name, ins):
                done[0] += 1
                assert jobs.of[name][1:] == ("scalar", done[0]), name
                ins.then_inc(by_scalar, 1)

            def copy(dst, src, scale=None):
                if scale is None:
                    return nc.scalar.activation(dst, src, ACT.Copy)
                return nc.scalar.activation(dst, src, ACT.Copy, scale=scale)

            act.wait_ge(consts_in, 3 * 16)
            nc.scalar.activation(CS, CS, ACT.Silu).then_inc(silu_c, 1)
            for l in range(DEPTH):
                for n in (0, 1):
                    act.wait_ge(sin_arg, 2 * l + n + 1)
                    nc.scalar.activation(FH[0:FHID, 2 + n, :], FH[0:FHID, 0, :], ACT.Sin).then_inc(sin_out, 1)

            def ada(l, c):
                b = filled(("ada", l, c))
                n = 12 * l + c
                if n >= 2:
                    act.wait_ge(row_sent[n % 2], 16 * (n // 2))
                drained(("ada", l, c), copy(MROW[:, n % 2, :], b[0:2, :]))

            for l in range(DEPTH):
                full = FULL[l]
                first = full[0] * P
                for c in range(4):
                    ada(l, c)
                for t in range(TILES):
                    b = filled(("hT", l, 1, t, 0))
                    drained(("hT", l, 1, t, 0), copy(HT[:, 0:4, t * P:(t + 1) * P], b[:, :].rearrange("p (k t) -> p k t", k=4)))
                for t in full:
                    b = filled(("q", l, t))
                    drained(("q", l, t), copy(QKV[:, t, 0:512].rearrange("p (c s d) -> p c s d", s=2, c=4),
                                              b[:, :].rearrange("p (s c d) -> p c s d", s=2, c=4)))
                for t in range(TILES):
                    drained(("kv", l, t), copy(QKV[:, t, 512:1024], filled(("kv", l, t))[:, :]))
                for f in range(4):
                    b = filled(("bqk", l, f))
                    lo = first if f < 2 else 0
                    drained(("bqk", l, f), copy(BQK[:, f, lo:HALF], b[:, lo:HALF], HEAD ** -0.5 if f < 2 else None))
                act.wait_ge(pads_ready, l + 1)
                for f in range(6):
                    b = filled(("c", l, f))
                    s0 = full[0] // 2
                    drained(("c", l, f), copy(CP[:, f, s0:2, 1:SEQ + 1],
                                              b[:, first:HALF].rearrange("p (s t) -> p s t", t=SEQ)))
                for c in range(4, 12):
                    ada(l, c)
                for t in range(TILES):
                    if t in full:
                        b = filled(("qT", l, t))
                        drained(("qT", l, t), copy(QA[:, :, t * P:(t + 1) * P], b[:, :].rearrange("p (c t) -> p c t", c=4)))
                    b = filled(("kT", l, t))
                    drained(("kT", l, t), copy(KA[:, t * P:(t + 1) * P], b[:, 0:P]))
                for t in full:
                    b = filled(("uT", l, t))
                    drained(("uT", l, t), copy(UT[:, t, :], b[:, 0:C_CH]))
                mine = units[l]
                n = len(mine)
                for i in range(n + S_AHEAD):
                    if i < n:
                        nk = len(mine[i][3]) * P
                        U = unit_base[l] + i
                        b = filled(("S", l, i))
                        act.wait_ge(max_ready, U + 1)
                        if i >= 2:
                            act.wait_ge(bank_filled, jobs.filled(("PT", l, i - 2)))
                        if U >= 4:
                            act.wait_ge(o_read, U - 3)
                        drained(("S", l, i), nc.scalar.activation(
                            PB[:, i % 2, 0:nk], b[:, 0:nk], ACT.Exp, bias=NM[:, U % 4:U % 4 + 1],
                            accum_out=SM[:, U % 4:U % 4 + 1]))
                    u = i - S_AHEAD
                    if u >= 0 and u % 2 == 1:
                        nk = len(mine[u][3]) * P
                        b = filled(("PT", l, u))
                        if u >= 2:
                            act.wait_ge(o_filled, unit_base[l] + u - 1)
                        drained(("PT", l, u), copy(PT[:, u % 2, 0:nk], b[:, 0:nk]))
                for t in full:
                    for h in (0, 1):
                        b = filled(("oT", l, t, h))
                        nch = 2 if h else 4
                        drained(("oT", l, t, h), copy(OT[:, 4 * h:4 * h + nch, t * P:(t + 1) * P],
                                                      b[:, 0:nch * P].rearrange("p (c t) -> p c t", c=nch)))
                base = TILES + (l * (TILES + len(FULL[0])))
                for g, t in enumerate(full):
                    act.wait_ge(h_ready, base + g + 1)
                    act.dma_start(h_dram[t * P:(t + 1) * P, :], HN[:, t, :]).then_inc(h_stored, 16)
                    b = filled(("hT", l, 2, t, 0))
                    drained(("hT", l, 2, t, 0), copy(HT[:, 0:4, t * P:(t + 1) * P], b[:, :].rearrange("p (k t) -> p k t", k=4)))
                b = filled(("rt", l))
                w = EXPERTS * len(full)
                drained(("rt", l), nc.scalar.activation(RT[:, 0, 0:w], b[:, 0:w], ACT.Exp, scale=-1.0))
                for g, t in enumerate(full):
                    n_ = len(FULL[0]) * l + g
                    b = filled(("sh", l, t))
                    if g >= 2:
                        act.wait_ge(sa_ready, n_ - 1)
                    nc.scalar.activation(SG[:, g % 2, :], b[:, 0:SHARED], ACT.Silu).then_inc(sg_ready, 1)
                for g, t in enumerate(full):
                    b = filled(("sT", l, t))
                    drained(("sT", l, t), copy(ST[:, g % 2, :, :], b[:, 0:2 * P].rearrange("p (c t) -> p c t", c=2)))
                    for h in (0, 1):
                        b = filled(("sy", l, t, h))
                        drained(("sy", l, t, h), copy(MACC[:, t, h * HALF:(h + 1) * HALF], b[:, :]))

                L = loop[l]
                act.wait_ge(zeros_ready, l + 1)
                act.sem_inc(L["y_scalar"], 1)
                act.sem_inc(L["y_out0"], 16)
                act.sem_inc(L["y_out1"], 16)
                act.wait_ge(rows_filled, 16)
                act.wait_ge(h_stored, 16 * (len(FULL[0]) * l + len(full)))
                act.wait_ge(list_ready, 2 * (l + 1))
                always, most = turns_of(l)
                blocks = act.value_load(LIST[0:1, BLOCKS_MAX:BLOCKS_MAX + 1], min_val=EXPERTS, max_val=UNROLL * most)
                turns = act.snap((blocks + UNROLL - 1) // UNROLL)

                def tokens_T(v):
                    copy(XGT[:, v, 0:4, :], XT_PS[0][:, 0:4 * SLOTS].rearrange("p (k t) -> p k t", k=4)).then_inc(L["xT_scalar"], 1)

                def act_T():
                    copy(ACTT[:, :], AT_PS[:, 0:SLOTS]).then_inc(L["actT"], 1)

                def second(b, w, stores):
                    act.wait_ge(L["y_ps"], b * 2 + 9)
                    act.wait_ge(L[f"y_out{w}"], stores * 16 + 16)
                    copy(YSB[0:SLOTS, w, 0:HALF], Y_PS[0][0:SLOTS, :]).then_inc(L["y_scalar"], 1)
                    act.wait_ge(L["y_scalar"], b + 2)
                    act.wait_ge(L["y_vector"], b + 2)
                    act.dma_start(y_dram[bass.ds(b, 1), :, :].rearrange("a s d -> (a s) d"),
                                  YSB[0:SLOTS, w, :]).then_inc(L[f"y_out{w}"], 16)

                def turn(i):
                    for u in range(UNROLL):
                        b = i * UNROLL + u
                        act.wait_ge(L["actT_ps"], b + 1)
                        act_T()
                        act.wait_ge(L["xT_ps"], b + 3)
                        tokens_T((u + 1) % 2)
                        act.wait_ge(L["ab_ps"], b + 1)
                        nc.scalar.activation(SIL[0:SLOTS, :], AB_PS[0:SLOTS, 0:HIDDEN], ACT.Silu).then_inc(L["silu"], 1)
                        second(b, (u + 1) % 2, i * 2 + u // 2)

                act.wait_ge(L["xT_ps"], 2)
                tokens_T(0)
                with act.Fori(0, always) as i:
                    turn(i)
                with act.Fori(always, most) as i:
                    with act.If(i < turns):
                        turn(i)
                total = act.snap(turns * UNROLL)
                act.wait_ge(L["actT_ps"], total + 1)
                act.wait_ge(L["actT_ps"], EXPERTS)
                act_T()
                second(total, 1, turns * 2)

        @block.vector
        def _(dve):
            done = [0]
            steps = [0]

            def link(ins):
                steps[0] += 1
                ins.then_inc(vector_step, 1)
                dve.wait_ge(vector_step, steps[0])

            def free(ins):
                steps[0] += 1
                ins.then_inc(vector_step, 1)

            def filled(name):
                dve.wait_ge(bank_filled, jobs.filled(name))
                return bank(name)

            def drained(name, ins):
                done[0] += 1
                assert jobs.of[name][1:] == ("vector", done[0]), name
                ins.then_inc(by_vector, 1)
                dve.wait_ge(by_vector, done[0])

            tt = dve.tensor_tensor
            ts = dve.tensor_scalar
            stt = dve.scalar_tensor_tensor

            def rsqrt(v, n, scale):
                x, y, w = NV[:, 0:n], RS[:, 0:n].bitcast(F32), NT[:, 0:n]
                link(ts(x, v, scale, EPS, ALU.mult, ALU.add))
                link(ts(RS[:, 0:n], x.bitcast(I32), -0.5, float(0x5F3759DF), ALU.mult, ALU.add))
                for _ in range(3):
                    link(tt(w, y, y, ALU.mult))
                    link(stt(w, w, -0.5, x, ALU.mult, ALU.mult))
                    link(stt(y, w, 1.5, y, ALU.add, ALU.mult))

            def normalise(tiles, out_):
                for t in tiles:
                    for h in (0, 1):
                        free(dve.bn_stats(out=STAT[:, t, 6 * h:6 * h + 6], in_=X[:, t, h * HALF:(h + 1) * HALF]))
                dve.wait_ge(vector_step, steps[0])
                for t in tiles:
                    free(dve.bn_aggr(out=MV[:, t, :], in_=STAT[:, t, :]))
                dve.wait_ge(vector_step, steps[0])
                rsqrt(MV[:, tiles[0]:tiles[-1] + 1, 1], len(tiles), 1.0)
                for g, t in enumerate(tiles):
                    free(ts(out_[:, t, :], X[:, t, :], MV[:, t, 0:1], RS[:, g:g + 1].bitcast(F32),
                            ALU.subtract, ALU.mult))
                dve.wait_ge(vector_step, steps[0])

            dve.wait_ge(consts_in, 3 * 16)
            dve.wait_ge(once_in, 7 * 16)
            dve.tensor_copy(TRI[:, :], ONCE_SB).then_inc(tables_ready, 1)
            for l in range(DEPTH):
                for n, name in enumerate((("fil1", l), ("fil2", l))):
                    b = filled(name)
                    arg, turns_ = FH[0:FHID, 0, :], FH[0:FHID, 1, :]
                    if l + n:
                        dve.wait_ge(sin_out, 2 * l + n)
                    drained(name, ts(arg, b[0:FHID, 0:SEQ], FCOL[:, l, 2 * n:2 * n + 1], FCOL[:, l, 2 * n + 1:2 * n + 2],
                                     ALU.add, ALU.mult))
                    link(ts(turns_, arg, 1.0 / (2 * math.pi), 12582912.0, ALU.mult, ALU.add))
                    link(ts(turns_, turns_, 12582912.0, None, ALU.subtract))
                    link(stt(arg, turns_, -6.28125, arg, ALU.mult, ALU.add))
                    link(stt(arg, turns_, -(2 * math.pi - 6.28125), arg, ALU.mult, ALU.add))
                    ts(arg, arg, 3.1415925, -3.1415925, ALU.min, ALU.max).then_inc(sin_arg, 1)
                for t in (0, 1):
                    b = filled(("fil3", l, t))
                    drained(("fil3", l, t), tt(FT[:, t, :], b[:, :], DECAY[:, t, :], ALU.mult))
                if l:
                    dve.wait_ge(bank_filled, jobs.filled(("filK", l - 1, 1, 1)))
                for t in (0, 1):
                    free(tt(FS[:, t, 0:C_CH], FT[:, t, 0:C_CH], FT[:, t, C_CH:2 * C_CH], ALU.add))
                    free(tt(FS[:, t, C_CH:2 * C_CH], FT[:, t, 0:C_CH], FT[:, t, C_CH:2 * C_CH], ALU.subtract))
                dve.wait_ge(vector_step, steps[0])
                dve.nop().then_inc(filt_ready, 1)
                for m in (0, 1):
                    for cs in (0, 1):
                        b = filled(("filK", l, m, cs))
                        drained(("filK", l, m, cs), dve.tensor_copy(KF[:, l, m, cs, :], b[:, 0:C_CH]))
            dve.wait_ge(x_in, 4 * 16)
            dve.wait_ge(small_in, 3 * 16)
            link(ts(GAIN[:, :, 0, :], GAIN[:, :, 0, :], HEAD ** -0.5, None, ALU.mult))

            for l in range(DEPTH):
                full = FULL[l]
                ns = len(full) // 2
                lo = full[0] * P

                def modulated(which, tiles):
                    normalise(tiles, HN)
                    dve.wait_ge(moda_in, 64 * (2 * l + which))
                    for t in tiles:
                        link(stt(HN[:, t, :], MODA[:, 1, t // 2, :], 1.0, HN[:, t, :], ALU.add, ALU.mult))
                        tt(HN[:, t, :], HN[:, t, :], MODA[:, 0, t // 2, :], ALU.add).then_inc(h_ready, 1)
                    for t in tiles:
                        b = filled(("hT", l, which, t, 1))
                        drained(("hT", l, which, t, 1), dve.tensor_copy(
                            HT[:, 4:8, t * P:(t + 1) * P], b[:, :].rearrange("p (k t) -> p k t", k=4)))
                    dve.nop().then_inc(moda_used, 1)

                modulated(1, tuple(range(TILES)))
                for e in (0, SEQ + 1):
                    free(dve.memset(CP[:, :, :, e:e + 1], 0.0))
                dve.wait_ge(vector_step, steps[0])
                dve.nop().then_inc(pads_ready, 1)

                dve.wait_ge(by_scalar, jobs.of[("kv", l, TILES - 1)][2])
                for t in range(TILES):
                    h0 = 0 if t in full else 8
                    src = QKV[:, t, 0:640].rearrange("p (h d) -> p h d", h=10)[:, h0:10, :]
                    link(tt(SQ[:, h0:10, :], src, src, ALU.mult))
                    link(dve.tensor_reduce(SS[:, 10 * t + h0:10 * t + 10], SQ[:, h0:10, :], AX.X, ALU.add))
                    if h0:
                        free(dve.memset(SS[:, 10 * t:10 * t + h0], 1.0))
                dve.wait_ge(vector_step, steps[0])
                rsqrt(SS[:, :], 40, 1.0 / HEAD)
                for t in range(TILES):
                    h0 = 0 if t in full else 8
                    n = 10 - h0
                    src = QKV[:, t, 0:640].rearrange("p (h d) -> p h d", h=10)
                    rs = RS[:, 10 * t + h0:10 * t + 10].bitcast(F32).unsqueeze(2).to_broadcast([P, n, HEAD])
                    link(tt(SQ[:, h0:10, :], src[:, h0:10, :], rs, ALU.mult))
                    dst = SQ if t >= 2 else QN[:, t]
                    if not h0:
                        free(tt(dst[:, 0:8, :], SQ[:, 0:8, :], GAIN[:, l, 0, :].unsqueeze(1).to_broadcast([P, 8, HEAD]), ALU.mult))
                    g = tt(dst[:, 8:10, :], SQ[:, 8:10, :], GAIN[:, l, 1, :].unsqueeze(1).to_broadcast([P, 2, HEAD]), ALU.mult)
                    if t < 2:
                        link(g)
                        dve.nop().then_inc(qn_ready, 1)
                        continue
                    link(g)
                    c = const("cos")[:, 32 * (t - 2):32 * (t - 1)].unsqueeze(1).to_broadcast([P, 10, 32])
                    s = const("sin")[:, 32 * (t - 2):32 * (t - 1)].unsqueeze(1).to_broadcast([P, 10, 32])
                    x1, x2 = SQ[:, :, 0:HEAD:2], SQ[:, :, 1:HEAD:2]
                    free(tt(RP[:, 0], x1, c, ALU.mult))
                    free(tt(RP[:, 1], x2, s, ALU.mult))
                    dve.wait_ge(vector_step, steps[0])
                    link(tt(QN[:, t, :, 0:HEAD:2], RP[:, 0], RP[:, 1], ALU.subtract))
                    free(tt(RP[:, 0], x1, s, ALU.mult))
                    free(tt(RP[:, 1], x2, c, ALU.mult))
                    dve.wait_ge(vector_step, steps[0])
                    tt(QN[:, t, :, 1:HEAD:2], RP[:, 0], RP[:, 1], ALU.add).then_inc(qn_ready, 1)
                    dve.wait_ge(qn_ready, TILES * l + t + 1)

                dve.wait_ge(by_scalar, jobs.of[("c", l, 5)][2])
                s0 = 2 - ns
                for f in range(6):
                    def w(i):
                        return HYC[:, l, 3 * f + i:3 * f + i + 1]
                    z = OT[:, f, lo:HALF].rearrange("p (s t) -> p s t", t=SEQ)
                    link(ts(z, CP[:, f, s0:2, 0:SEQ], w(0), HYC[:, l, 18 + f:19 + f], ALU.mult, ALU.add))
                    link(stt(z, CP[:, f, s0:2, 1:SEQ + 1], w(1), z, ALU.mult, ALU.add))
                    link(stt(z, CP[:, f, s0:2, 2:SEQ + 2], w(2), z, ALU.mult, ALU.add))
                link(tt(OT[:, 2:4, lo:HALF], OT[:, 2:4, lo:HALF], OT[:, 4:6, lo:HALF], ALU.mult))
                dve.nop().then_inc(u_ready, 1)
                T1, T2 = PT[:, 0, 0:ns * C_CH], PT[:, 1, 0:ns * C_CH]
                T1, T2 = (x.rearrange("p (s c) -> p s c", s=ns) for x in (T1, T2))
                for m in (0, 1):
                    kc, ks = (KF[:, l, m, cs, :].unsqueeze(1).to_broadcast([P, ns, C_CH]) for cs in (0, 1))
                    yc, ys = (YF[:, m, cs, 0:ns * C_CH].rearrange("p (s c) -> p s c", s=ns) for cs in (0, 1))
                    b = filled(("U", l, m, 0))[:, 0:ns * C_CH].rearrange("p (s c) -> p s c", s=ns)
                    link(tt(yc, b, kc, ALU.mult))
                    drained(("U", l, m, 0), tt(ys, b, ks, ALU.mult))
                    b = filled(("U", l, m, 1))[:, 0:ns * C_CH].rearrange("p (s c) -> p s c", s=ns)
                    link(tt(T1, b, ks, ALU.mult))
                    drained(("U", l, m, 1), tt(T2, b, kc, ALU.mult))
                    link(tt(yc, yc, T1, ALU.subtract))
                    tt(ys, ys, T2, ALU.add).then_inc(yf_ready, 1)
                    dve.wait_ge(yf_ready, 2 * l + m + 1)
                for ct in (0, 1):
                    b = filled(("yh", l, ct))
                    t1 = PT[:, 0, 0:ns * SEQ]
                    link(stt(t1, OT[:, 2 + ct, lo:HALF], HYC[:, l, 24 + ct:25 + ct], b[:, 0:ns * SEQ], ALU.mult, ALU.add))
                    drained(("yh", l, ct), tt(OT[:, 6 + ct, lo:HALF], t1, OT[:, ct, lo:HALF], ALU.mult))

                n = item_at[("mixc", l)]
                dve.wait_ge(ring_in[n % RING], sum(48 if x[0] == "wo" else 32 for x in items[n % RING:n + 1:RING]))
                bias = item(("mixc", l))[:, 8 * SEQ:16 * SEQ].rearrange("p (t h c) -> p t h c", t=2, h=B_HEADS)
                dve.wait_ge(mask_in, 16 * (l + 1))
                mask = MASK_SB
                for t in (0, 1):
                    for h2 in range(2):
                        ins = tt(bias[:, t, 2 * h2:2 * h2 + 2, :], bias[:, t, 2 * h2:2 * h2 + 2, :],
                                 mask[:, t, :].unsqueeze(1).to_broadcast([P, 2, SEQ]), ALU.add)
                        link(ins)
                mine = units[l]
                n = len(mine)
                for i in range(n + S_AHEAD + PV_LAG):
                    if i < n:
                        t, kind, h, keys = mine[i]
                        nk = len(keys) * P
                        U = unit_base[l] + i
                        b = filled(("S", l, i))
                        if kind == "B" and t >= 2:
                            link(tt(b[:, 2 * P:4 * P], b[:, 2 * P:4 * P], bias[:, t - 2, h, :], ALU.add))
                        if i >= 4:
                            dve.wait_ge(by_scalar, jobs.of[("S", l, i - 4)][2])
                        dve.tensor_reduce(NM[:, U % 4:U % 4 + 1], b[:, 0:nk], AX.X, ALU.max, negate=True).then_inc(max_ready, 1)
                    u = i - S_AHEAD
                    if 0 <= u < n and u % 2 == 0:
                        nk = len(mine[u][3]) * P
                        b = filled(("PT", l, u))
                        if u >= 2:
                            dve.wait_ge(o_filled, unit_base[l] + u - 1)
                        drained(("PT", l, u), dve.tensor_copy(PT[:, u % 2, 0:nk], b[:, 0:nk]))
                    u = i - S_AHEAD - PV_LAG
                    if 0 <= u < n:
                        t, kind, h, keys = mine[u]
                        U = unit_base[l] + u
                        dve.wait_ge(by_scalar, jobs.of[("S", l, u)][2])
                        link(dve.reciprocal(RC[:, U % 4:U % 4 + 1], SM[:, U % 4:U % 4 + 1]))
                        dve.wait_ge(o_filled, U + 1)
                        col = 64 * (2 * (h % 4) + h // 4) if kind == "A" else 512 + 64 * h
                        ts(OTOK[:, t, col:col + 64], O_BANK[U % 2][:, 0:HEAD],
                           RC[:, U % 4:U % 4 + 1], None, ALU.mult).then_inc(o_read, 1)
                dve.nop().then_inc(bias_used, 1)

                dve.wait_ge(modg_in, 32 * (2 * l + 1))
                for t in full:
                    for h in (0, 1):
                        cols = slice(h * HALF, (h + 1) * HALF)
                        b = filled(("wo", l, t, h))
                        tmp = PB[:, h, :]
                        drained(("wo", l, t, h), tt(tmp, b[:, :], MODG[:, t // 2, cols], ALU.mult))
                        link(stt(X[:, t, cols], X[:, t, cols], ALPHA, tmp, ALU.mult, ALU.add))
                dve.nop().then_inc(modg_used, 1)

                def post_norm(which):
                    normalise(full, X)
                    dve.wait_ge(norm_in, 32 * (2 * l + which))
                    for t in full:
                        link(tt(X[:, t, :], X[:, t, :], LNB[:, 0, :], ALU.mult))
                        link(tt(X[:, t, :], X[:, t, :], LNB[:, 1, :], ALU.add))
                    dve.nop().then_inc(norm_used, 1)

                post_norm(1)
                modulated(2, full)

                W_ = EXPERTS * len(full)
                nt = len(full)

                def R(i, w=W_):
                    return RT[:, i, 0:w]

                def R3(i):
                    return R(i).rearrange("p (t e) -> p t e", t=nt)
                dve.wait_ge(by_scalar, jobs.of[("rt", l)][2])
                link(ts(R(0), R(0), 1.0, None, ALU.add))
                link(dve.reciprocal(R(0), R(0)))
                link(tt(R3(1), R3(0), RB[:, l, :].unsqueeze(1).to_broadcast([P, nt, EXPERTS]), ALU.add))
                G = nt * GROUPS
                sel8 = R(1).rearrange("p (g e) -> p g e", e=8)
                hi4, lo4 = (RT[:, 2, o:o + 4 * G].rearrange("p (g e) -> p g e", e=4) for o in (0, 128))
                hi2, lo2, m2 = (RT[:, 3, o:o + 2 * G].rearrange("p (g e) -> p g e", e=2) for o in (0, 64, 128))
                hi1, lo1, m1 = (RT[:, 4, o:o + G].rearrange("p (g e) -> p g e", e=1) for o in (0, 32, 64))
                free(tt(hi4, sel8[:, :, 0:4], sel8[:, :, 4:8], ALU.max))
                link(tt(lo4, sel8[:, :, 0:4], sel8[:, :, 4:8], ALU.min))
                for (hi, lo_), (hi_, lo__, mid), w in (((hi4, lo4), (hi2, lo2, m2), 2), ((hi2, lo2), (hi1, lo1, m1), 1)):
                    free(tt(hi_, hi[:, :, 0:w], hi[:, :, w:2 * w], ALU.max))
                    free(tt(mid, hi[:, :, 0:w], hi[:, :, w:2 * w], ALU.min))
                    link(tt(lo__, lo_[:, :, 0:w], lo_[:, :, w:2 * w], ALU.max))
                    link(tt(lo__, lo__, mid, ALU.max))
                gs = RT[:, 4, 96:96 + G].rearrange("p (t g) -> p t g", t=nt)
                link(tt(gs.rearrange("p t g -> p (t g)"), hi1.rearrange("p g e -> p (g e)"), lo1.rearrange("p g e -> p (g e)"), ALU.add))
                mine_ = gs.unsqueeze(3).to_broadcast([P, nt, 8, 8])
                others = gs.unsqueeze(2).to_broadcast([P, nt, 8, 8])
                gt = R(2).rearrange("p (t g h) -> p t g h", t=nt, g=8)
                eq = R(3).rearrange("p (t g h) -> p t g h", t=nt, g=8)
                before = const("before8").rearrange("p (g h) -> p g h", g=8).unsqueeze(1).to_broadcast([P, nt, 8, 8])
                link(tt(gt, others, mine_, ALU.is_gt))
                link(tt(eq, others, mine_, ALU.is_equal))
                link(tt(eq, eq, before, ALU.mult))
                link(tt(R(2), R(2), R(3), ALU.add))
                rank = RT[:, 4, 0:G]
                link(dve.tensor_reduce(rank, R(2).rearrange("p (g h) -> p g h", h=8), AX.X, ALU.add))
                link(ts(rank, rank, TOP_GROUPS - 0.5, MASKED, ALU.is_gt, ALU.mult))
                link(tt(R(1).rearrange("p (g e) -> p g e", e=8), sel8, rank.unsqueeze(2).to_broadcast([P, G, 8]), ALU.add))
                for g in range(nt):
                    free(dve.max(out=P8[:, g, :], in_=R3(1)[:, g, :]))
                dve.wait_ge(vector_step, steps[0])
                for g in range(nt):
                    free(dve.match_replace(out=R3(2)[:, g, :], in_to_replace=P8[:, g, :], in_values=R3(1)[:, g, :],
                                           imm_value=-3e38))
                dve.wait_ge(vector_step, steps[0])
                M16 = RT[:, 10, :].bitcast(BF16)[:, 0:W_]
                link(tt(R(3), R(2), R(1), ALU.not_equal))
                dve.tensor_copy(M16, R(3)).then_inc(mask_ready, 1)
                dve.wait_ge(mask_ready, l + 1)
                link(tt(R(0), R(0), R(3), ALU.mult))
                ws = NT[:, 0:nt]
                link(dve.tensor_reduce(ws, R3(0), AX.X, ALU.add))
                link(dve.reciprocal(ws, ws))
                link(ts(ws, ws, ROUTED_SCALE, None, ALU.mult))
                link(tt(R3(0), R3(0), ws.unsqueeze(2).to_broadcast([P, nt, EXPERTS]), ALU.mult))

                def shared_act(g, t):
                    n_ = len(FULL[0]) * l + g
                    b = filled(("sh", l, t))
                    dve.wait_ge(sg_ready, n_ + 1)
                    drained(("sh", l, t), tt(SAW[:, t, 0:SHARED], SG[:, g % 2, :], b[:, SHARED:2 * SHARED], ALU.mult))
                    dve.nop().then_inc(sa_ready, 1)

                for g in range(nt - 1):
                    shared_act(g, full[g])
                NB16 = RT[:, 11, :].bitcast(BF16)
                b = filled(("count", l))
                drained(("count", l), dve.tensor_copy(NB1[0:EXPERTS, 0:1], b[0:EXPERTS, 0:1]))
                link(ts(NB1[0:EXPERTS, 1:2], NB1[0:EXPERTS, 0:1], SLOTS + 0.5, 1.0, ALU.is_gt, ALU.add))
                for j in range(2, -(-P * nt // SLOTS)):
                    link(stt(NB1[0:EXPERTS, 1:2], NB1[0:EXPERTS, 0:1], j * SLOTS + 0.5, NB1[0:EXPERTS, 1:2], ALU.is_gt, ALU.add))
                link(dve.tensor_copy(NB16[0:EXPERTS, 0:1], NB1[0:EXPERTS, 1:2]))
                ts(NB16[0:EXPERTS, 128:256], table("ones", EXPERTS), NB1[0:EXPERTS, 1:2], None, ALU.mult).then_inc(nb_ready, 1)
                b = filled(("ends", l))
                drained(("ends", l), dve.tensor_copy(NB1[0:EXPERTS, 2:3], b[0:EXPERTS, 0:1]))
                ts(NB16[0:EXPERTS, 256:256 + BLOCKS_MAX], const("iota_block")[0:EXPERTS, :], NB1[0:EXPERTS, 2:3], None,
                   ALU.is_ge).then_inc(ends_ready, 1)
                b = filled(("list", l))
                ts(LIST[0:1, 0:BLOCKS_MAX], b[0:1, 0:BLOCKS_MAX], float(EXPERTS - 1), None, ALU.min).then_inc(list_ready, 1)
                drained(("list", l), dve.tensor_copy(LIST[0:1, BLOCKS_MAX:BLOCKS_MAX + 1], b[0:1, BLOCKS_MAX:BLOCKS_MAX + 1]))
                dve.nop().then_inc(list_ready, 1)
                b = filled(("pos", l))
                drained(("pos", l), stt(R(5), b[:, 0:W_], 1.0, R(3), ALU.add, ALU.mult))
                for g in range(nt):
                    free(dve.max(out=P8[:, g, :], in_=R3(5)[:, g, :]))
                dve.wait_ge(vector_step, steps[0])
                p8 = P8[:, 0:nt, :].rearrange("p t j -> p (t j)")
                n8 = nt * TOP_K
                slot_i, block_i = PSB[:, 0, 0:n8], PSB[:, 1, 0:n8]
                slot_f, block_f = PSB[:, 2, 0:n8].bitcast(F32), PSB[:, 3, 0:n8].bitcast(F32)
                link(ts(slot_i, p8, 1.0, None, ALU.subtract))
                link(ts(block_i, slot_i, int(math.log2(SLOTS)), None, ALU.logical_shift_right))
                link(ts(slot_i, slot_i, SLOTS - 1, None, ALU.bitwise_and))
                link(dve.tensor_copy(slot_f, slot_i))
                link(dve.tensor_copy(block_f, block_i))
                for n_ in range(n8):
                    N_ = n_ + l * TOP_K * len(FULL[0])
                    t = full[n_ // TOP_K]
                    if n_ >= 4:
                        dve.wait_ge(onehot_used, n_ - 3 + l * (TOP_K * len(FULL[0]) - 1))
                    free(ts(ONE_S[:, N_ % 4, :], const("iota_slot"), slot_f[:, n_:n_ + 1], None, ALU.is_equal))
                    ts(ONE_B[:, N_ % 4, :], const("iota_block"), block_f[:, n_:n_ + 1],
                       const("token")[:, t:t + 1], ALU.is_equal, ALU.mult).then_inc(onehot, 1)
                    dve.wait_ge(vector_step, steps[0])
                b = filled(("idx", l))
                drained(("idx", l), dve.tensor_copy(IDX[0:SLOTS, :], b[0:SLOTS, 0:BLOCKS_MAX]))
                dve.nop().then_inc(idx_ready, 1)
                shared_act(nt - 1, full[-1])
                link(ts(POSI[:, 0:nt, :].rearrange("p t j -> p (t j)"), p8, float(SLOTS - 1), None, ALU.add))
                for g in range(nt):
                    for j in range(TOP_K):
                        free(stt(RT[:, 6, 0:EXPERTS], R3(5)[:, g, :], P8[:, g, j:j + 1], R3(0)[:, g, :], ALU.is_equal, ALU.mult,
                                 accum_out=G8[:, g, j:j + 1]))
                        dve.wait_ge(vector_step, steps[0])
                dve.nop().then_inc(choices_ready, 1)

                L = loop[l]
                link(dve.memset(ACTV[:, :], 0.0))
                dve.wait_ge(bank_filled, jobs.filled(last_job(("sw2", l))))
                link(dve.memset(expert_w(UNROLL - 1)[1], 0.0))
                dve.nop().then_inc(zeros_ready, 1)
                dve.sem_inc(L["act"], 1)
                dve.sem_inc(L["y_vector"], 1)
                dve.wait_ge(h_stored, 16 * (len(FULL[0]) * l + nt))
                always, most = turns_of(l)
                blocks = dve.value_load(LIST[0:1, BLOCKS_MAX:BLOCKS_MAX + 1], min_val=EXPERTS, max_val=UNROLL * most)
                turns = dve.snap((blocks + UNROLL - 1) // UNROLL)

                def tokens_T(v):
                    dve.tensor_copy(XGT[:, v, 4:8, :], XT_PS[1][:, 0:4 * SLOTS].rearrange("p (k t) -> p k t", k=4)).then_inc(L["xT_vector"], 1)

                def second(b, w, stores):
                    dve.wait_ge(L["y_ps"], b * 2 + 10)
                    dve.wait_ge(L[f"y_out{w}"], stores * 16 + 16)
                    dve.tensor_copy(YSB[0:SLOTS, w, HALF:D], Y_PS[1][0:SLOTS, :]).then_inc(L["y_vector"], 1)

                def turn(i):
                    for u in range(UNROLL):
                        b = i * UNROLL + u
                        dve.wait_ge(L["xT_ps"], b + 3)
                        tokens_T((u + 1) % 2)
                        dve.wait_ge(L["silu"], b + 1)
                        tt(ACTV[0:SLOTS, :], SIL[0:SLOTS, :], AB_PS[0:SLOTS, HIDDEN:2 * HIDDEN], ALU.mult).then_inc(L["act"], 1)
                        second(b, (u + 1) % 2, i * 2 + u // 2)

                dve.wait_ge(L["xT_ps"], 2)
                tokens_T(0)
                with dve.Fori(0, always) as i:
                    turn(i)
                with dve.Fori(always, most) as i:
                    with dve.If(i < turns):
                        turn(i)
                second(dve.snap(turns * UNROLL), 1, turns * 2)

                dve.wait_ge(by_scalar, jobs.of[("sy", l, full[-1], 1)][2])
                base = l * len(FULL[0]) * TOP_K
                for n_ in range(nt * TOP_K):
                    t = full[n_ // TOP_K]
                    N_ = base + n_
                    dve.wait_ge(gathered[N_ % 4], 16 * (N_ // 4 + 1))
                    stt(MACC[:, t, :], YG[N_ % 4], G8[:, n_ // TOP_K, n_ % TOP_K:n_ % TOP_K + 1], MACC[:, t, :],
                        ALU.mult, ALU.add).then_inc(choice_used, 1)
                    dve.wait_ge(choice_used, N_ + 1)
                dve.wait_ge(modg_in, 32 * (2 * l + 2))
                for t in full:
                    link(tt(MACC[:, t, :], MACC[:, t, :], MODG[:, t // 2, :], ALU.mult))
                    link(stt(X[:, t, :], X[:, t, :], ALPHA, MACC[:, t, :], ALU.mult, ALU.add))
                dve.nop().then_inc(modg_used, 1)
                post_norm(2)
            for _ in FULL[-1]:
                dve.nop().then_inc(out_ready, 1)

        @block.gpsimd
        def _(pool):
            def load(dst, src, s):
                pool.dma_start(dst, src).then_inc(s, 16)

            def row(src):
                return src.partition_broadcast(P)

            for l in range(DEPTH):
                for v in (0, 1):
                    load(mod_dram[l, v:v + 1, :], a["ada_b"][l:l + 1, :], bias_rows)
            pool.wait_ge(bias_rows, 64)
            load(GAIN[:, :, 0, :], a["q_gain"].partition_broadcast(P), small_in)
            load(GAIN[:, :, 1, :], a["k_gain"].partition_broadcast(P), small_in)
            load(RB, a["router_b"].partition_broadcast(P), small_in)

            def send(l, c):
                n = 12 * l + c
                pool.wait_ge(by_scalar, jobs.of[("ada", l, c)][2])
                pool.dma_start(mod_dram[l, :, c * HALF:(c + 1) * HALF], MROW[:, n % 2, :],
                               accum_op=ALU.add).then_inc(row_sent[n % 2], 16)

            def sent(l, c):
                n = 12 * l + c
                pool.wait_ge(row_sent[0], 16 * (n // 2 + 1))
                pool.wait_ge(row_sent[1], 16 * ((n + 1) // 2))

            def part(l, i, v):
                return mod_dram[l, v, i * D:(i + 1) * D].partition_broadcast(P)

            def shift_scale(l, which):
                for w in (0, 1):
                    for v in (0, 1):
                        load(MODA[:, w, v, :], part(l, 3 * (which - 1) + w, v), moda_in)

            def gates(l, which):
                for v in (0, 1):
                    load(MODG[:, v, :], part(l, 3 * which - 1, v), modg_in)

            def norm_rows(l, which):
                load(LNB[:, 0, :], a[f"ln{which}_g"][l].partition_broadcast(P), norm_in)
                load(LNB[:, 1, :], a[f"ln{which}_b"][l].partition_broadcast(P), norm_in)

            for l in range(DEPTH):
                full = FULL[l]
                nt = len(full)
                for c in range(4):
                    send(l, c)
                sent(l, 3)
                if l:
                    pool.wait_ge(moda_used, 2 * l)
                shift_scale(l, 1)
                if l:
                    pool.wait_ge(norm_used, 2 * l)
                norm_rows(l, 1)
                pool.wait_ge(moda_used, 2 * l + 1)
                load(MASK_SB, a["mask"], mask_in)
                for c in range(4, 12):
                    send(l, c)
                sent(l, 11)
                if l:
                    pool.wait_ge(modg_used, 2 * l)
                gates(l, 1)
                shift_scale(l, 2)
                pool.wait_ge(norm_used, 2 * l + 1)
                norm_rows(l, 2)
                pool.wait_ge(modg_used, 2 * l + 1)
                gates(l, 2)

                L = loop[l]
                pool.wait_ge(idx_ready, l + 1)
                pool.wait_ge(h_stored, 16 * (len(FULL[0]) * l + nt))
                pool.wait_ge(list_ready, 2 * (l + 1))
                always, most = turns_of(l)
                blocks = pool.value_load(LIST[0:1, BLOCKS_MAX:BLOCKS_MAX + 1], min_val=EXPERTS, max_val=UNROLL * most)
                turns = pool.snap((blocks + UNROLL - 1) // UNROLL)

                def gather(b, v, copies):
                    pool.tensor_copy(IDXB[0:SLOTS, v:v + 1], IDX[0:SLOTS, bass.ds(b, 1)]).then_inc(L["index_copied"], 1)
                    pool.wait_ge(L["index_copied"], copies)
                    pool.wait_ge(idx_ready, l + 1)
                    pool.sem_inc(L["gathers"], 1)
                    nc.gpsimd.indirect_dma_start(
                        out=XG[0:SLOTS, v, :], out_offset=None, in_=h_dram,
                        in_offset=bass.IndirectOffsetOnAxis(ap=IDXB[0:SLOTS, v:v + 1].bitcast(U32), axis=0)).then_inc(L[f"x_in{v}"], 16)

                def turn(i):
                    for u in range(UNROLL):
                        b = i * UNROLL + u
                        pool.wait_ge(L["xT_ps"], b + 1)
                        pool.wait_ge(idx_ready, l + 1)
                        gather(b + 1, (u + 1) % 2, b + 2)

                gather(0, 0, 1)
                with pool.Fori(0, always) as i:
                    turn(i)
                with pool.Fori(always, most) as i:
                    with pool.If(i < turns):
                        turn(i)
                pool.wait_ge(L["y_out0"], turns * (8 * UNROLL) + 16)
                pool.wait_ge(L["y_out1"], turns * (8 * UNROLL) + 32)
                pool.wait_ge(L["y_ps"], turns * (2 * UNROLL) + 10)
                pool.wait_ge(L["xT_scalar"], turns * UNROLL + 1)
                pool.wait_ge(L["xT_vector"], turns * UNROLL + 1)
                pool.wait_ge(choices_ready, l + 1)
                pool.nop().then_inc(y_sent, 1)
                base = l * len(FULL[0]) * TOP_K
                for n_ in range(nt * TOP_K):
                    N_ = base + n_
                    if n_ >= 4:
                        pool.wait_ge(choice_used, N_ - 3)
                    nc.gpsimd.indirect_dma_start(
                        out=YG[N_ % 4], out_offset=None, in_=y_dram.rearrange("b s d -> (b s) d"),
                        in_offset=bass.IndirectOffsetOnAxis(ap=POSI[:, n_ // TOP_K, n_ % TOP_K:n_ % TOP_K + 1].bitcast(U32), axis=0)
                    ).then_inc(gathered[N_ % 4], 16)


def kernel(**inputs):
    import concourse.bacc as bacc
    from concourse.bass_utils import run_bass_kernel_spmd

    x = {k: np.asarray(v) for k, v in inputs.items()}
    L = DEPTH

    def columns(v, n):
        return np.moveaxis(v.reshape(v.shape[:-1] + (n, P)), -1, 0)

    arrays = dict(constants())
    arrays["x"], arrays["ctx"] = x["x"][0], x["ctx"][0]
    arrays["cond"] = np.stack([x["c_ctx"], x["c"][0]], -1).reshape(P, KD, 2)
    taps = columns(x["hy_conv_w"].transpose(0, 1, 2), 6)
    arrays["hyc"] = np.concatenate([taps.transpose(0, 1, 3, 2).reshape(P, L, 18), columns(x["hy_conv_b"], 6),
                                    columns(x["hy_skip"], 2)], -1)
    arrays["f_w1"] = x["hy_f_w1"].transpose(1, 0, 2)
    arrays["f_w2"] = x["hy_f_w2"].transpose(1, 0, 2)
    arrays["f_w3"] = x["hy_f_w3"].transpose(1, 0, 2)
    arrays["f_col"] = np.stack([x["hy_f_b1"], x["hy_freq"][:, 0], x["hy_f_b2"], x["hy_freq"][:, 1]], -1).transpose(1, 0, 2)
    t = np.arange(SEQ)
    dr = t[None, :] // GRID_W - t[:, None] // GRID_W + 7
    dc = np.clip(t[None, :] % GRID_W - t[:, None] % GRID_W + 15, 0, 30)
    arrays["rpb"] = x["nat_rpb"][:, :, dr, dc].reshape(L, B_HEADS, 2, P, SEQ).transpose(0, 3, 2, 1, 4).reshape(L, P, 8 * SEQ)
    for n in ("ada_w", "ada_b", "w_in", "q_gain", "k_gain", "w_out", "ln1_g", "ln1_b", "ln2_g", "ln2_b", "router_w",
              "router_b", "exp_w1", "exp_w3", "exp_w2", "sh_w1", "sh_w3", "sh_w2"):
        arrays[n] = x[n]
    nc = bacc.Bacc("TRN2", target_bir_lowering=False, num_devices=1)
    feed, aps = {}, {}
    for n, v in arrays.items():
        v = np.ascontiguousarray(v)
        feed[f"in_{n}"] = v
        aps[n] = nc.dram_tensor(f"in_{n}", v.shape, mybir.dt.from_np(v.dtype), kind="ExternalInput").ap()
    out = nc.dram_tensor("out_latent", (SEQ, D), F32, kind="ExternalOutput").ap()
    scratch = (nc.dram_tensor("scratch_h", (TILES * P, D), F32).ap(),
               nc.dram_tensor("scratch_y", (BLOCKS_MAX + 1, SLOTS, D), F32).ap(),
               nc.dram_tensor("scratch_mod", (DEPTH, 2, 6 * D), F32).ap())
    hybrid_backbone(nc, aps, out, scratch)
    r = run_bass_kernel_spmd(nc, [feed], core_ids=[0])
    return r.results[0]["out_latent"].reshape(1, SEQ, D)
```

```python
import math
from contextlib import ExitStack

import concourse.bass as bass
import numpy as np
from concourse import mybir

F32 = mybir.dt.float32
BF16 = mybir.dt.bfloat16
F32R = mybir.dt.float32r
I32 = mybir.dt.int32
U32 = mybir.dt.uint32
ALU = mybir.AluOpType
ACT = mybir.ActivationFunctionType
AX = mybir.AxisListType

P = 128
DEPTH = 2
D = 1024
KD = D // P
SEQ = 256
GRID_W = 64
HEAD = 64
A_HEADS, A_KV, B_HEADS = 8, 2, 4
A_W, A_KV_W, B_W, C_CH = 512, 128, 256, 256
A_K0 = A_W
B_Q0 = A_K0 + 2 * A_KV_W
B_V0 = B_Q0 + 2 * B_W
C0 = B_V0 + B_W
MIX = A_W + B_W + C_CH
EXPERTS, TOP_K, GROUPS, TOP_GROUPS, HIDDEN, SHARED = 64, 8, 8, 4, 128, 256
ROUTED_SCALE = 2.5
ALPHA = (2 * DEPTH) ** 0.25
EPS = 1e-6
BANDS = 16
POS = 2 * BANDS + 1
FHID = 64
HALF = 512
TILES = 4
STREAMS = ((0, 1), (2, 3))
FULL = ((0, 1, 2, 3), (2, 3))
SLOTS = (128, 64)
UNROLL = 4
RING = 3
MASKED = -1e30
ROTATING = 6


def turns_of(l):
    tokens = P * len(FULL[l])
    worst = EXPERTS + (tokens * TOP_K - EXPERTS) // SLOTS[l]
    return EXPERTS // UNROLL, -(-worst // UNROLL)


AHEAD = 3
BLOCKS_MAX = UNROLL * max(turns_of(l)[1] for l in range(DEPTH)) + UNROLL
EMPTY = 8192

CONST = {}
_at = 0
for _n, _w in (("ident", P), ("cos", 2 * 32), ("sin", 2 * 32), ("iota_slot", P), ("iota_block", BLOCKS_MAX),
               ("before8", 64), ("choice", TILES * TOP_K), ("pick", 4)):
    CONST[_n] = (_at, _at + _w)
    _at += _w
CONST_W = _at
ONCE = {}
_at = 0
for _n, _w in (("before128", P), ("ones", P), ("start64", EXPERTS), ("upto64", EXPERTS)):
    ONCE[_n] = (_at, _at + _w)
    _at += _w
ONCE_W = _at


def constants():
    t = np.arange(SEQ)
    half = HEAD // 2
    inv = (10000.0 ** (-np.arange(0, half, 2, dtype=np.float32) / half)).astype(np.float32)
    ang = np.concatenate([(t // GRID_W).astype(np.float32)[:, None] * inv,
                          (t % GRID_W).astype(np.float32)[:, None] * inv], -1).astype(np.float32)
    tab = np.zeros((P, CONST_W), np.float32)

    def put(a, table, name, v):
        a[:, table[name][0]:table[name][1]] = v

    put(tab, CONST, "ident", np.eye(P))
    put(tab, CONST, "cos", np.cos(ang).reshape(2, P, 32).transpose(1, 0, 2).reshape(P, 64))
    put(tab, CONST, "sin", np.sin(ang).reshape(2, P, 32).transpose(1, 0, 2).reshape(P, 64))
    put(tab, CONST, "iota_slot", np.arange(P))
    put(tab, CONST, "iota_block", np.arange(BLOCKS_MAX))
    g = np.arange(GROUPS)
    put(tab, CONST, "before8", (g[None, :] < g[:, None]).reshape(1, 64))
    put(tab, CONST, "choice", (
        1 + (np.arange(TILES)[None, :, None] * P + np.arange(P)[:, None, None]) * TOP_K
        + np.arange(TOP_K)).reshape(P, TILES * TOP_K))
    put(tab, CONST, "pick", np.eye(2).reshape(1, 4))
    once = np.zeros((P, ONCE_W), np.float32)
    i = np.arange(P)
    e = np.arange(EXPERTS)
    put(once, ONCE, "before128", i[:, None] < i[None, :])
    put(once, ONCE, "ones", 1.0)
    once[:EXPERTS, ONCE["start64"][0]:ONCE["start64"][1]] = e[:, None] < e[None, :]
    once[:EXPERTS, ONCE["upto64"][0]:ONCE["upto64"][1]] = e[:, None] <= e[None, :]
    theta = 2 * np.pi * (np.arange(SEQ) + 0.5) / (2 * SEQ)
    c, s = np.cos(np.outer(t, theta)), np.sin(np.outer(t, theta))
    fwd = np.stack([c.reshape(2, P, SEQ), s.reshape(2, P, SEQ)], 1)
    inv_ = np.stack([c.T.reshape(2, P, SEQ), s.T.reshape(2, P, SEQ)], 1) / SEQ
    dft = np.stack([fwd, inv_]).transpose(3, 0, 1, 2, 4).reshape(P, 8 * SEQ).astype(np.float32)
    col = t % GRID_W
    first = np.clip(col - 8, 0, GRID_W - 16)
    inside = (col[None, :] >= first[:, None]) & (col[None, :] < first[:, None] + 16)
    mask = np.where(inside, 0.0, MASKED).astype(np.float32).reshape(2, P, SEQ).transpose(1, 0, 2)
    tt = np.linspace(0.0, 1.0, SEQ, dtype=np.float32)[:, None]
    w = (2 * math.pi * np.arange(SEQ, dtype=np.float32)[:, None] / SEQ).astype(np.float32)
    f = np.linspace(1e-4, BANDS - 1, BANDS, dtype=np.float32)[None]
    z = np.concatenate([tt, np.cos(f * w), -np.sin(f * w)], -1).astype(np.float32).T
    lo, hi = math.log(1e-2) / 1.5, math.log(1e-2) / 0.3
    deltas = np.abs(np.linspace(lo, hi, C_CH, dtype=np.float32))
    decay = np.exp(-tt * deltas[None]).astype(np.float32)
    back = decay.copy()
    back[0] = 0.0
    both = np.stack([decay, back], 1).reshape(2, P, 2 * C_CH).transpose(1, 0, 2)
    return {"tab": tab, "once": once, "dft": dft, "mask": np.ascontiguousarray(mask),
            "pos": np.ascontiguousarray(z), "decay": np.ascontiguousarray(both)}


class Banks:

    def __init__(self):
        self.order, self.of, self.read = [], {}, {"scalar": 0, "vector": 0}

    def add(self, name, reader):
        self.read[reader] += 1
        self.of[name] = (len(self.order), reader, self.read[reader])
        self.order.append(name)

    def filled(self, name):
        return self.of[name][0] + 1

    def before(self, name):
        j = self.of[name][0] - ROTATING
        return self.of[self.order[j]][1:] if j >= 0 else None


def attention_units():
    units = []
    for l in range(DEPTH):
        mine = []
        for t in FULL[l]:
            keys = (0, 1) if t < 2 else (0, 1, 2, 3)
            mine += [(t, "A", h, keys) for h in (0, 4, 1, 5, 2, 6, 3, 7)]
            mine += [(t, "B", h, keys) for h in range(B_HEADS)]
        units.append(mine)
    return units


ADA_VECTOR = (4, 5, 6, 7)
ADA_EARLY = 3
ADA_LATE = 10
S_AHEAD, PV_LAG = 2, 1


def plan():
    jobs, units = Banks(), attention_units()
    for l in range(DEPTH):
        jobs.add(("fil1", l), "vector")
        if l == 0:
            jobs.add(("ada", 0, 0), "scalar")
        jobs.add(("fil2", l), "vector")
        if l == 0:
            jobs.add(("ada", 0, 1), "scalar")
        for tt in (0, 1):
            jobs.add(("fil3", l, tt), "vector")
        if l == 0:
            jobs.add(("ada", 0, 2), "scalar")
            jobs.add(("ada", 0, 3), "scalar")
        for m in (0, 1):
            for cs in (0, 1):
                jobs.add(("filK", l, m, cs), "vector")
    for l in range(DEPTH):
        full = FULL[l]
        for c in range(ADA_EARLY, ADA_LATE if l else 0):
            jobs.add(("ada", l, c), "scalar")
        for t in range(TILES):
            for h in (0, 1):
                jobs.add(("hT", l, 1, t, h), ("scalar", "vector")[h])
        for t in full:
            jobs.add(("q", l, t), "scalar")
        if l == 0:
            jobs.add(("ada", l, ADA_VECTOR[0]), "scalar")
        for t in range(TILES):
            jobs.add(("kv", l, t), "scalar")
        if l == 0:
            jobs.add(("ada", l, ADA_VECTOR[1]), "scalar")
        for f in range(4):
            jobs.add(("bqk", l, f), "scalar")
        if l == 0:
            jobs.add(("ada", l, ADA_VECTOR[2]), "scalar")
        for f in range(6):
            jobs.add(("c", l, f), "scalar")
        if l == 0:
            jobs.add(("ada", l, ADA_VECTOR[3]), "scalar")
        for c in range(8, 12 if l == 0 else 0):
            jobs.add(("ada", l, c), "scalar")
        for t in range(TILES):
            if t in full:
                jobs.add(("qT", l, t), "scalar")
            jobs.add(("kT", l, t), "scalar")
        for t in full:
            jobs.add(("uT", l, t), "scalar")
        for m in (0, 1):
            for cs in (0, 1):
                jobs.add(("U", l, m, cs), "vector")
        for ct in (0, 1):
            jobs.add(("yh", l, ct), "vector")
        n = len(units[l])
        for i in range(n + S_AHEAD + PV_LAG):
            if i < n:
                jobs.add(("S", l, i), "scalar")
            if 0 <= i - S_AHEAD < n:
                u = i - S_AHEAD
                jobs.add(("PT", l, u), ("vector", "scalar")[u % 2])
        for t in full:
            for h in (0, 1):
                jobs.add(("oT", l, t, h), "scalar")
        for t in full:
            for h in (0, 1):
                jobs.add(("wo", l, t, h), "vector")
        for c in AFTER_OUT[l]:
            jobs.add(("ada", 1, c), "scalar")
        for t in full:
            for h in (0, 1):
                jobs.add(("hT", l, 2, t, h), ("scalar", "vector")[h])
        jobs.add(("rt", l), "scalar")
        for t in full[:-1]:
            jobs.add(("sh", l, t), "vector")
        jobs.add(("count", l), "vector")
        jobs.add(("ends", l), "vector")
        jobs.add(("list", l), "vector")
        jobs.add(("pos", l), "vector")
        jobs.add(("sh", l, full[-1]), "vector")
        for t in full:
            jobs.add(("sT", l, t), "scalar")
            for h in (0, 1):
                jobs.add(("sy", l, t, h), "scalar")
    return jobs, units


AFTER_OUT = (range(ADA_EARLY), range(ADA_LATE, 12))


def last_job(it):
    kind, l = it[0], it[1]
    return {"dft": ("filK", DEPTH - 1, 1, 1), "ada": it, "mixc": ("yh", l, 1), "wo": ("wo", l, TILES - 1, 1),
            "sw13": ("sh", l, TILES - 1), "sw2": ("sy", l, TILES - 1, 1),
            "win": (("q", l, TILES - 1), ("kv", l, TILES - 1), ("bqk", l, 3), ("c", l, 3), ("c", l, 5))[it[-1] if kind == "win" else 0]}[kind]


def weight_items():
    items = [("ada", 0, 0), ("ada", 0, 1), ("dft", 0), ("ada", 0, 2), ("ada", 0, 3)]
    for l in range(DEPTH):
        items += [("ada", l, c) for c in range(ADA_EARLY, ADA_LATE if l else 0)]
        for b in range(5):
            items += [("win", l, b)] + [("ada", l, c) for c in ADA_VECTOR[b:b + 1] if l == 0]
        items += [("ada", l, c) for c in range(8, 12 if l == 0 else 0)]
        items += [("mixc", l), ("wo", l, 0), ("wo", l, 1)]
        items += [("ada", 1, c) for c in AFTER_OUT[l]]
        items += [("sw13", l), ("sw2", l)]
    return items


def hybrid_backbone(nc, a, out, scratch):
    jobs, units = plan()
    items = weight_items()
    item_at = {it: n for n, it in enumerate(items)}
    unit_base = (0, len(units[0]))
    ada_order = [x[1:] for x in jobs.order if x[0] == "ada"]
    with ExitStack() as ctx:
        def sb(name, cols, dt=F32, rows=P):
            return ctx.enter_context(nc.sbuf_tensor(name, [rows, cols], dt))

        def sem(name):
            return ctx.enter_context(nc.semaphore(name))

        X = sb("residual", TILES * D)[:, :].rearrange("p (t d) -> p t d", t=TILES)
        HN = sb("tokens_h", TILES * D)[:, :].rearrange("p (t d) -> p t d", t=TILES)
        HT = sb("features_h", KD * HALF)[:, :].rearrange("p (k t) -> p k t", k=KD)
        QKV = sb("qkv", TILES * D)[:, :].rearrange("p (t d) -> p t d", t=TILES)
        BQK_ = sb("b_qk", 4 * HALF)
        CP_ = sb("c_padded", 6 * 2 * (SEQ + 2))
        QA_ = sb("a_q", 4 * HALF)
        KA0 = sb("a_k", HALF)
        MODA = sb("shift_scale", 4 * D)[:, :].rearrange("p (w v d) -> p w v d", w=2, v=2)
        MODG = sb("gate_rows", 2 * D)[:, :].rearrange("p (v d) -> p v d", v=2)
        LNB = sb("norm_rows", 2 * D)[:, :].rearrange("p (w d) -> p w d", w=2)
        WB = sb("weights", RING * 4096)
        KF = sb("filters", DEPTH * 4 * C_CH)[:, :].rearrange("p (l m s c) -> p l m s c", l=DEPTH, m=2, s=2)
        TAB = sb("tab", CONST_W)
        GAIN = sb("gains", DEPTH * 2 * HEAD)[:, :].rearrange("p (l w d) -> p l w d", l=DEPTH, w=2)
        HYC = sb("hyena_columns", DEPTH * 26)[:, :].rearrange("p (l c) -> p l c", l=DEPTH)
        MROW = sb("mod_rows", 2 * HALF, rows=2)[:, :].rearrange("p (s c) -> p s c", s=2)
        RW = sb("router_w", KD * EXPERTS)[:, :].rearrange("p (k e) -> p k e", k=KD)
        RB = sb("router_b", DEPTH * EXPERTS)[:, :].rearrange("p (l e) -> p l e", l=DEPTH)
        PB = sb("probs", 2 * HALF)[:, :].rearrange("p (s c) -> p s c", s=2)
        PT = sb("probs_T", 2 * HALF)[:, :].rearrange("p (s c) -> p s c", s=2)
        ONE_S = sb("onehot_slot", 2 * P, F32R)[:, :].rearrange("p (s c) -> p s c", s=2)
        ONE_B = sb("onehot_block", 2 * BLOCKS_MAX, F32R)[:, :].rearrange("p (s c) -> p s c", s=2)
        TRI = sb("count_tables", ONCE_W, BF16)
        SIL = sb("silu_a", HIDDEN)
        ACTV = sb("expert_act", HIDDEN)
        ACTT = sb("expert_act_T", P)
        CS = sb("silu_c", KD * 2)[:, :].rearrange("p (k v) -> p k v", k=KD)
        STAT = sb("stats", TILES * 12)[:, :].rearrange("p (t c) -> p t c", t=TILES)
        MV = sb("mean_var", TILES * 2)[:, :].rearrange("p (t c) -> p t c", t=TILES)
        RS = sb("rstd", 40, I32)
        NV = sb("newton_v", 40)
        NT = sb("newton_t", 40)
        SS = sb("square_sums", 40)
        NM = sb("neg_max", 4)
        SM = sb("prob_sum", 4)
        RC = sb("prob_recip", 4)
        P8 = sb("choice_keys", TILES * 8)[:, :].rearrange("p (t j) -> p t j", t=TILES)
        G8 = sb("choice_gates", TILES * 8)[:, :].rearrange("p (t j) -> p t j", t=TILES)
        PSB = sb("slot_and_block", 4 * TILES * 8, I32)[:, :].rearrange("p (w c) -> p w c", w=4)
        TOKEN = sb("token_of_slot", BLOCKS_MAX, I32)
        CHOICE = sb("choice_of_slot", BLOCKS_MAX + 1, I32)
        IDXB = sb("gather_index", UNROLL, I32)
        IDYB = sb("scatter_index", UNROLL, I32)
        LIST = sb("block_experts", BLOCKS_MAX + 1, I32, rows=1)
        NB1 = sb("block_counts", 8)

        BQK = BQK_[:, :].rearrange("p (f t) -> p f t", f=4)
        CP = CP_[:, :].rearrange("p (f s t) -> p f s t", f=6, s=2)
        QA = QA_[:, :].rearrange("p (c t) -> p c t", c=4)
        KP = QKV[:, :, 0:640].rearrange("p t (n c) -> p n t c", n=5)
        OT = HT
        QN = HN[:, 0:3, :].rearrange("p t d -> p (t d)")[:, 0:4 * 640].rearrange("p (t h d) -> p t h d", t=4, h=10)
        MASK_SB = HN[:, 2, 512:1024].rearrange("p (t c) -> p t c", t=2)
        SQ = HN[:, 3, 0:640].rearrange("p (h d) -> p h d", h=10)
        RP = PT.rearrange("p s c -> p (s c)")[:, 0:640].rearrange("p (w h d) -> p w h d", w=2, h=10)
        ACC = PB, PT
        OTOK = HN
        MACC = QKV
        UT = CP_[:, 0:4 * C_CH].rearrange("p (t c) -> p t c", t=4)
        YF = CP_[:, 4 * C_CH:4 * C_CH + 4 * HALF].rearrange("p (m s c) -> p m s c", m=2, s=2)
        XG = MODA.rearrange("p w v d -> p (w v) d")
        XGT = BQK_[:, :].rearrange("p (s k t) -> p s k t", s=2, k=KD)
        YSB = HN
        RT = CP_[:, 0:12 * 256].rearrange("p (a c) -> p a c", a=12)
        SG = PB.rearrange("p s c -> p (s c)")[:, 0:2 * SHARED].rearrange("p (s c) -> p s c", s=2)
        SAW = QKV
        ST = PT.rearrange("p s c -> p (s c)")[:, 0:4 * P].rearrange("p (s h t) -> p s h t", s=2, h=2)
        YG = [x.rearrange("p (j d) -> p j d", j=2) for x in (
            QA_[:, :], BQK_[:, :], HT[:, 0:4, :].rearrange("p k t -> p (k t)"), HT[:, 4:8, :].rearrange("p k t -> p (k t)"))]
        SPARE = CP_[:, 7 * 256:7 * 256 + BLOCKS_MAX]
        ONCE_SB = QKV[:, 0, 0:ONCE_W]
        POS_SB = QKV[0:POS, 1, 0:SEQ]
        FW1 = QKV[0:POS, 1, SEQ:SEQ + DEPTH * FHID].rearrange("p (l c) -> p l c", l=DEPTH)
        FW2 = QKV[0:FHID, 1, 384:384 + DEPTH * FHID].rearrange("p (l c) -> p l c", l=DEPTH)
        FCOL = QKV[0:FHID, 1, 512:512 + DEPTH * 4].rearrange("p (l c) -> p l c", l=DEPTH)
        FW3 = QKV[0:FHID, 2, :].rearrange("p (l c) -> p l c", l=DEPTH)
        DECAY = QKV[:, 3, :].rearrange("p (t c) -> p t c", t=2)
        FH = HT[:, 0:4, 0:SEQ]
        FT = HT[:, 4:6, :]
        FS = HT[:, 6:8, :]

        def const(name):
            return TAB[:, CONST[name][0]:CONST[name][1]]

        def table(name, rows=P):
            return TRI[0:rows, ONCE[name][0]:ONCE[name][1]]

        ident = const("ident")

        def ring(n):
            return WB[:, (n % RING) * 4096:(n % RING + 1) * 4096]

        def item(it):
            return ring(item_at[it])

        def ring_arrivals(n):
            return sum(48 if x[0] == "wo" else 32 for x in items[n % RING:n + 1:RING])

        def expert_w(u):
            r = WB[:, u * 3072:(u + 1) * 3072]
            return r[:, 0:2048].rearrange("p (m k h) -> p m k h", m=2, k=KD), r[:, 2048:3072]

        PS = [ctx.enter_context(nc.psum_tensor(f"bank{i}", [P, HALF], F32)) for i in range(8)]
        O_BANK = PS[6:8]
        XT_PS, AB_PS, AT_PS, Y_PS = PS[0:2], PS[2], PS[3], PS[4:6]

        def bank(name):
            return PS[jobs.of[name][0] % ROTATING]

        consts_in = sem("consts_in")
        once_in = sem("once_in")
        x_in = sem("x_in")
        ring_in = [sem(f"ring_in{i}") for i in range(RING)]
        bias_used = sem("window_bias_used")
        mask_in = sem("mask_in")
        small_in = sem("small_rows_in")
        router_in = sem("router_in")
        bank_filled = sem("bank_filled")
        by_scalar = sem("read_by_scalar")
        by_vector = sem("read_by_vector")
        vector_step = sem("vector_step")
        silu_c = sem("silu_c_ready")
        sin_arg = sem("sin_arg_ready")
        sin_out = sem("sin_ready")
        filt_ready = sem("filter_sums_ready")
        tables_ready = sem("tables_ready")
        row_sent = [sem(f"mod_row_sent{i}") for i in range(2)]
        bias_rows = sem("mod_bias_in_dram")
        moda_in = sem("shift_scale_in")
        modg_in = sem("gate_rows_in")
        norm_in = sem("norm_rows_in")
        moda_used = sem("shift_scale_used")
        modg_used = sem("gate_rows_used")
        norm_used = sem("norm_rows_used")
        h_ready = sem("h_ready")
        h_stored = sem("h_stored")
        qn_ready = sem("qk_normed")
        u_ready = sem("hyena_u_ready")
        yf_ready = sem("hyena_product_ready")
        pads_ready = sem("pads_ready")
        partial_sums = sem("partial_sums_ready")
        keys_padded = sem("keys_padded")
        max_ready = sem("neg_max_ready")
        o_filled = sem("attention_product_done")
        o_read = sem("attention_output_ready")
        mask_ready = sem("choice_ready")
        nb_ready = sem("block_counts_ready")
        ends_ready = sem("block_ends_ready")
        onehot = sem("onehots_ready")
        onehot_used = sem("onehots_used")
        list_ready = sem("block_list_ready")
        sg_ready = sem("shared_silu_ready")
        sa_ready = sem("shared_act_ready")
        idx_ready = sem("token_list_ready")
        zeros_ready = sem("dummy_block_ready")
        gathered = [sem(f"choice_gathered{i}") for i in range(4)]
        choice_used = sem("choice_added")
        y_sent = sem("expert_rows_in_dram")
        out_ready = sem("output_ready")
        out_sent = sem("output_sent")
        loop = [{n: sem(f"{n}_{l}") for n in (
            "w_in0", "w_in1", "w_in2", "w_in3", "x_in0", "x_in1", "x_in2", "x_in3", "y_out0", "y_out1", "y_out2",
            "y_out3", "indices_copied", "moves", "started",
            "xT_ps", "xT_scalar", "xT_vector", "ab_ps", "silu", "act", "actT_ps", "actT", "y_ps", "y_scalar",
            "y_vector")} for l in range(DEPTH)]

        h_dram, y_dram, mod_dram = scratch
        y_rows = y_dram.rearrange("(t p j) d -> t p j d", p=P, j=TOP_K)
        block = ctx.enter_context(nc.Block())

        @block.sync
        def _(sp):
            def load(dst, src, s, inc=16):
                sp.dma_start(dst, src).then_inc(s, inc)

            load(TAB[:, :], a["tab"], consts_in)
            load(CS, a["cond"], consts_in)
            load(HYC, a["hyc"], consts_in)
            load(ONCE_SB, a["once"], once_in)
            load(POS_SB, a["pos"], once_in)
            load(FW1, a["f_w1"], once_in)
            load(FW2, a["f_w2"], once_in)
            load(FCOL, a["f_col"], once_in)
            load(FW3, a["f_w3"], once_in)
            load(DECAY, a["decay"], once_in)

            def ring_load(n):
                it = items[n]
                if n >= RING:
                    sp.wait_ge(bank_filled, jobs.filled(last_job(items[n - RING])))
                if n >= RING and items[n - RING][0] == "mixc":
                    sp.wait_ge(bias_used, items[n - RING][1] + 1)
                s, kind, dst = ring_in[n % RING], it[0], ring(n)
                if kind == "dft":
                    load(dst[:, 0:4 * SEQ], a["dft"][:, 0:4 * SEQ], s, 32)
                elif kind == "ada":
                    load(dst.rearrange("p (k c) -> p k c", k=KD),
                         a["ada_w"][it[1]].rearrange("(p k) c -> p k c", k=KD)[:, :, it[2] * HALF:(it[2] + 1) * HALF],
                         s, 32)
                elif kind == "win":
                    w = a["w_in"][it[1]].rearrange("(p k) c -> p k c", k=KD)
                    d = dst.rearrange("p (k c) -> p k c", k=KD)
                    parts = {0: [(0, 0, 512)], 1: [(0, A_K0, 256), (256, B_V0, 256)], 2: [(0, B_Q0, 512)],
                             3: [(0, C0, 512)], 4: [(0, C0 + 512, 256)]}[it[2]]
                    for at, c, n_ in parts:
                        load(d[:, :, at:at + n_], w[:, :, c:c + n_], s, 32 // len(parts))
                elif kind == "mixc":
                    load(dst[:, 0:8 * SEQ], a["dft"], s)
                    load(dst[:, 8 * SEQ:16 * SEQ], a["rpb"][it[1]], s)
                elif kind == "wo":
                    w = a["w_out"][it[1]]
                    d = dst.rearrange("p (c n) -> p c n", c=KD)
                    cols = slice(it[2] * HALF, (it[2] + 1) * HALF)
                    for s_ in (0, 1):
                        load(d[64 * s_:64 * s_ + 64, 0:4, :],
                             w[256 * s_:256 * s_ + 256, cols].rearrange("(c d) n -> d c n", c=4), s, 16)
                    load(d[:, 4:8, :], w[512:1024, cols].rearrange("(c p) n -> p c n", p=P), s, 16)
                elif kind == "sw13":
                    d = dst.rearrange("p (m k c) -> p m k c", m=2, k=KD)
                    for m, name in ((0, "sh_w1"), (1, "sh_w3")):
                        load(d[:, m], a[name][it[1]].rearrange("(p k) c -> p k c", k=KD), s)
                elif kind == "sw2":
                    load(dst[:, 0:2 * D].rearrange("p (c n) -> p c n", c=2),
                         a["sh_w2"][it[1]].rearrange("(c p) n -> p c n", p=P), s, 32)

            def rows_back(l, n):
                full = FULL[l]
                g, j = divmod(2 * n, TOP_K)
                N = l * len(FULL[0]) * TOP_K // 2 + n
                if n >= len(YG):
                    sp.wait_ge(choice_used, N - len(YG) + 1)
                load(YG[N % 4], y_rows[full[g]][:, j:j + 2, :], gathered[N % 4])

            at = 0
            for l in range(DEPTH):
                last = item_at[("sw2", l)]
                if l:
                    pairs = len(FULL[l - 1]) * TOP_K // 2
                    ring_load(at)
                    at += 1
                    sp.wait_ge(y_sent, l)
                    for n in range(pairs):
                        rows_back(l - 1, n)
                        if n % 3 == 2:
                            ring_load(at)
                            at += 1
                while at <= last:
                    if items[at] == ("ada", 0, 2):
                        for t in range(TILES):
                            src = a["ctx"] if t < 2 else a["x"]
                            load(X[:, t, :], src[(t % 2) * P:(t % 2 + 1) * P, :], x_in)
                    ring_load(at)
                    at += 1
                    if items[at - 1][0] == "mixc":
                        if l >= 1:
                            sp.wait_ge(bank_filled, jobs.filled(("rt", l - 1)))
                        load(RW, a["router_w"][l].rearrange("(p k) e -> p k e", k=KD), router_in)
                L, S = loop[l], SLOTS[l]
                sp.wait_ge(bank_filled, jobs.filled(last_job(("sw2", l))))
                sp.wait_ge(list_ready, 2 * (l + 1))
                always, most = turns_of(l)
                blocks = sp.value_load(LIST[0:1, BLOCKS_MAX:BLOCKS_MAX + 1], min_val=EXPERTS, max_val=UNROLL * most)
                turns = sp.snap((blocks + UNROLL - 1) // UNROLL)

                def turn(i):
                    for u in range(UNROLL):
                        b = i * UNROLL + u
                        e = sp.value_load(LIST[0:1, bass.ds(b, 1)], min_val=0, max_val=EXPERTS - 1)
                        sp.wait_ge(L["y_ps"], b * 2 + 4)
                        w13, w2 = expert_w(u)
                        for m, name in ((0, "exp_w1"), (1, "exp_w3")):
                            load(w13[:, m], a[name][l][bass.ds(e, 1), :, :].rearrange("a (p k) h -> (a p) k h", k=KD),
                                 L[f"w_in{u}"])
                        load(w2, a["exp_w2"][l][bass.ds(e, 1), :, :].rearrange("a h d -> (a h) d"), L[f"w_in{u}"])

                with sp.Fori(0, always) as i:
                    turn(i)
                with sp.Fori(always, most) as i:
                    with sp.If(i < turns):
                        turn(i)
                sp.wait_ge(L["y_ps"], turns * (2 * UNROLL) + 10)
            sp.wait_ge(y_sent, DEPTH)
            for n in range(len(FULL[-1]) * TOP_K // 2):
                rows_back(DEPTH - 1, n)
            for t in FULL[-1]:
                sp.wait_ge(out_ready, t - 1)
                sp.dma_start(out[(t % 2) * P:(t % 2 + 1) * P, :], X[:, t, :]).then_inc(out_sent, 16)
            sp.wait_ge(out_sent, 16 * len(FULL[-1]))

        @block.tensor
        def _(pe):
            waited = {"scalar": by_scalar, "vector": by_vector}

            def start(name):
                was = jobs.before(name)
                if was:
                    pe.wait_ge(waited[was[0]], was[1])
                return bank(name)

            def read_out(name):
                _, who, n = jobs.of[name]
                pe.wait_ge(waited[who], n)

            def arrived(it):
                n = item_at[it]
                pe.wait_ge(ring_in[n % RING], ring_arrivals(n))
                return item(it)

            pe.wait_ge(once_in, 7 * 16)
            def ada(l, c):
                w = arrived(("ada", l, c)).rearrange("p (k c) -> p k c", k=KD)
                b = start(("ada", l, c))
                for k in range(KD):
                    mm = pe.matmul(b[0:2, :], CS[:, k, :], w[:, k, :], start=k == 0, stop=k == KD - 1)
                mm.then_inc(bank_filled, 1)

            def summed(n):
                pe.wait_ge(partial_sums, n + 1)
                b = start(("ada", 0, ADA_VECTOR[n]))
                for v in (0, 1):
                    mm = pe.matmul(b[0:2, :], const("pick")[:, 2 * v:2 * v + 2], ACC[n % 2][:, v, :], start=v == 0, stop=v == 1)
                mm.then_inc(bank_filled, 1)

            for l in range(DEPTH):
                b = start(("fil1", l))
                pe.matmul(b[0:FHID, 0:SEQ], FW1[:, l, :], POS_SB, start=True, stop=True).then_inc(bank_filled, 1)
                if l == 0:
                    pe.wait_ge(silu_c, 1)
                    ada(0, 0)
                b = start(("fil2", l))
                pe.wait_ge(sin_out, 2 * l + 1)
                pe.matmul(b[0:FHID, 0:SEQ], FW2[:, l, :], FH[0:FHID, 2, :], start=True, stop=True).then_inc(bank_filled, 1)
                if l == 0:
                    ada(0, 1)
                pe.wait_ge(sin_out, 2 * l + 2)
                for tt in (0, 1):
                    b = start(("fil3", l, tt))
                    pe.matmul(b[:, :], FH[0:FHID, 3, tt * P:(tt + 1) * P], FW3[:, l, :], start=True,
                              stop=True).then_inc(bank_filled, 1)
                if l == 0:
                    ada(0, 2)
                    ada(0, 3)
                    dft0 = arrived(("dft", 0))[:, 0:4 * SEQ].rearrange("p (t s m) -> p t s m", t=2, s=2)
                pe.wait_ge(filt_ready, l + 1)
                for m in (0, 1):
                    for cs in (0, 1):
                        b = start(("filK", l, m, cs))
                        for tt in (0, 1):
                            mm = pe.matmul(b[:, 0:C_CH], dft0[:, tt, cs, m * P:(m + 1) * P],
                                           FS[:, tt, cs * C_CH:(cs + 1) * C_CH], start=tt == 0, stop=tt == 1)
                        mm.then_inc(bank_filled, 1)
            read_out(("filK", DEPTH - 1, 1, 1))

            def transposed_h(l, which, t, n):
                pe.wait_ge(h_ready, n)
                for h in (0, 1):
                    b = start(("hT", l, which, t, h))
                    for k in range(4):
                        mm = pe.transpose(b[:, k * P:(k + 1) * P], HN[:, t, 4 * h + k:D:KD], ident)
                    mm.then_inc(bank_filled, 1)

            h_count = 0
            for l in range(DEPTH):
                full = FULL[l]
                for c in range(ADA_EARLY, ADA_LATE if l else 0):
                    ada(l, c)
                for t in range(TILES):
                    h_count += 1
                    transposed_h(l, 1, t, h_count)
                for h in (0, 1):
                    read_out(("hT", l, 1, TILES - 1, h))
                w = arrived(("win", l, 0)).rearrange("p (k c) -> p k c", k=KD)
                for t in full:
                    b = start(("q", l, t))
                    for k in range(KD):
                        mm = pe.matmul(b[:, :], HT[:, k, t * P:(t + 1) * P], w[:, k, :], start=k == 0, stop=k == KD - 1)
                    mm.then_inc(bank_filled, 1)
                if l == 0:
                    summed(0)
                w = arrived(("win", l, 1)).rearrange("p (k c) -> p k c", k=KD)
                for t in range(TILES):
                    b = start(("kv", l, t))
                    for k in range(KD):
                        mm = pe.matmul(b[:, :], HT[:, k, t * P:(t + 1) * P], w[:, k, :], start=k == 0, stop=k == KD - 1)
                    mm.then_inc(bank_filled, 1)
                if l == 0:
                    summed(1)
                first = full[0] * P
                w = arrived(("win", l, 2)).rearrange("p (k c) -> p k c", k=KD)
                for f in range(4):
                    lo = first if f < 2 else 0
                    b = start(("bqk", l, f))
                    for k in range(KD):
                        mm = pe.matmul(b[:, lo:HALF], w[:, k, f * P:(f + 1) * P], HT[:, k, lo:HALF],
                                       start=k == 0, stop=k == KD - 1)
                    mm.then_inc(bank_filled, 1)
                if l == 0:
                    summed(2)
                for f in range(6):
                    w = arrived(("win", l, 3 + f // 4)).rearrange("p (k c) -> p k c", k=KD)
                    b = start(("c", l, f))
                    for k in range(KD):
                        mm = pe.matmul(b[:, first:HALF], w[:, k, (f % 4) * P:(f % 4 + 1) * P], HT[:, k, first:HALF],
                                       start=k == 0, stop=k == KD - 1)
                    mm.then_inc(bank_filled, 1)
                if l == 0:
                    summed(3)
                for c in range(8, 12 if l == 0 else 0):
                    ada(l, c)
                for t in range(TILES):
                    pe.wait_ge(qn_ready, TILES * l + t + 1)
                    if t in full:
                        b = start(("qT", l, t))
                        for c in range(4):
                            mm = pe.transpose(b[:, c * P:(c + 1) * P], QN[:, t, 2 * c:2 * c + 2, :].rearrange("p h d -> p (h d)"), ident)
                        mm.then_inc(bank_filled, 1)
                    b = start(("kT", l, t))
                    pe.transpose(b[:, 0:P], QN[:, t, 8:10, :].rearrange("p h d -> p (h d)"), ident).then_inc(bank_filled, 1)
                pe.wait_ge(u_ready, l + 1)
                for t in full:
                    b = start(("uT", l, t))
                    for ct in (0, 1):
                        mm = pe.transpose(b[:, ct * P:(ct + 1) * P], OT[:, 2 + ct, t * P:(t + 1) * P], ident)
                    mm.then_inc(bank_filled, 1)
                read_out(("uT", l, full[-1]))
                mixc = arrived(("mixc", l))
                fwd = mixc[:, 0:4 * SEQ].rearrange("p (t s m) -> p t s m", t=2, s=2)
                inv = mixc[:, 4 * SEQ:8 * SEQ].rearrange("p (m s t) -> p m s t", m=2, s=2)
                ns = len(full) // 2
                uts = UT.rearrange("p (s t) c -> p t s c", t=2)
                for m in (0, 1):
                    for cs in (0, 1):
                        b = start(("U", l, m, cs))
                        for tt in (0, 1):
                            mm = pe.matmul(b[:, 0:ns * C_CH].rearrange("p (s c) -> p s c", s=ns),
                                           fwd[:, tt, cs, m * P:(m + 1) * P], uts[:, tt, 2 - ns:2, :],
                                           start=tt == 0, stop=tt == 1)
                        mm.then_inc(bank_filled, 1)
                pe.wait_ge(yf_ready, 2 * (l + 1))
                for ct in (0, 1):
                    b = start(("yh", l, ct))
                    for s in range(ns):
                        for m in (0, 1):
                            for cs in (0, 1):
                                mm = pe.matmul(b[:, s * SEQ:(s + 1) * SEQ],
                                               YF[:, m, cs, s * C_CH + ct * P:s * C_CH + (ct + 1) * P],
                                               inv[:, m, cs, :], start=m + cs == 0, stop=m + cs == 2)
                    mm.then_inc(bank_filled, 1)
                for t in range(TILES):
                    if t in full:
                        read_out(("qT", l, t))
                    read_out(("kT", l, t))

                mine = units[l]
                n = len(mine)
                pe.wait_ge(keys_padded, 13 * (l + 1))

                def scores(u):
                    t, kind, h, keys = mine[u]
                    nk = len(keys) * P
                    b = start(("S", l, u))
                    if kind == "A":
                        q = QA[:, h % 4, t * P:(t + 1) * P]
                        k = KP[:, 0, 0:len(keys)] if h // 4 else KA0[:, 0:nk].rearrange("p (t c) -> p t c", c=P)
                    else:
                        q, k = BQK[:, h // 2, t * P:(t + 1) * P], KP[:, 1 + h, 0:len(keys)]
                    pe.matmul(b[:, 0:nk].rearrange("p (t c) -> p t c", c=P), q, k,
                              start=True, stop=True).then_inc(bank_filled, 1)

                def transposed(u):
                    keys = mine[u][3]
                    read_out(("S", l, u))
                    b = start(("PT", l, u))
                    for kt in keys:
                        mm = pe.transpose(b[:, kt * P:(kt + 1) * P], PB[:, u % 2, kt * P:(kt + 1) * P], ident)
                    mm.then_inc(bank_filled, 1)

                def product(u):
                    t, kind, h, keys = mine[u]
                    read_out(("PT", l, u))
                    U = unit_base[l] + u
                    if U >= 2:
                        pe.wait_ge(o_read, U - 1)
                    o = O_BANK[U % 2][:, 0:HEAD]
                    v0 = 640 + 64 * (h // 4) if kind == "A" else 768 + 64 * h
                    for kt in keys:
                        mm = pe.matmul(o, PT[:, u % 2, kt * P:(kt + 1) * P], QKV[:, kt, v0:v0 + 64],
                                       start=kt == keys[0], stop=kt == keys[-1])
                    mm.then_inc(o_filled, 1)

                for i in range(n + S_AHEAD + PV_LAG):
                    if i < n:
                        scores(i)
                    if 0 <= i - S_AHEAD < n:
                        transposed(i - S_AHEAD)
                    if 0 <= i - S_AHEAD - PV_LAG < n:
                        product(i - S_AHEAD - PV_LAG)
                pe.wait_ge(o_read, unit_base[l] + n)
                for t in full:
                    for h in (0, 1):
                        b = start(("oT", l, t, h))
                        for c in range(4 * h, 6 if h else 4):
                            mm = pe.transpose(b[:, (c % 4) * P:(c % 4 + 1) * P], OTOK[:, t, c * P:(c + 1) * P], ident)
                        mm.then_inc(bank_filled, 1)
                read_out(("oT", l, full[-1], 1))
                read_out(("yh", l, 1))
                pe.wait_ge(yf_ready, 2 * (l + 1))
                wo = [arrived(("wo", l, h)).rearrange("p (c n) -> p c n", c=KD) for h in (0, 1)]
                for t in full:
                    for h in (0, 1):
                        b = start(("wo", l, t, h))
                        for c in range(KD):
                            mm = pe.matmul(b[:, :], OT[:, c, t * P:(t + 1) * P], wo[h][:, c, :],
                                           start=c == 0, stop=c == KD - 1)
                        mm.then_inc(bank_filled, 1)

                for c in AFTER_OUT[l]:
                    ada(1, c)

                for t in full:
                    h_count += 1
                    transposed_h(l, 2, t, h_count)
                for h in (0, 1):
                    read_out(("hT", l, 2, full[-1], h))
                pe.wait_ge(router_in, 16 * (l + 1))
                b = start(("rt", l))
                for g, t in enumerate(full):
                    for k in range(KD):
                        mm = pe.matmul(b[:, g * EXPERTS:(g + 1) * EXPERTS], HT[:, k, t * P:(t + 1) * P], RW[:, k, :],
                                       start=k == 0, stop=k == KD - 1)
                mm.then_inc(bank_filled, 1)
                sw13 = arrived(("sw13", l)).rearrange("p (m k c) -> p m k c", m=2, k=KD)

                def shared_in(t):
                    b = start(("sh", l, t))
                    for k in range(KD):
                        mm = pe.matmul(b[:, :].rearrange("p (m c) -> p m c", m=2), HT[:, k, t * P:(t + 1) * P],
                                       sw13[:, :, k, :], start=k == 0, stop=k == KD - 1)
                    mm.then_inc(bank_filled, 1)

                for t in full[:-1]:
                    shared_in(t)
                M16 = RT[:, 10, :].bitcast(BF16)
                NB16 = RT[:, 11, :].bitcast(BF16)
                pe.wait_ge(tables_ready, 1)
                pe.wait_ge(mask_ready, l + 1)
                b = start(("count", l))
                for g in range(len(full)):
                    mm = pe.matmul(b[0:EXPERTS, 0:1], M16[:, g * EXPERTS:(g + 1) * EXPERTS], table("ones")[:, 0:1],
                                   start=g == 0, stop=g == len(full) - 1)
                mm.then_inc(bank_filled, 1)
                pe.wait_ge(nb_ready, l + 1)
                b = start(("ends", l))
                pe.matmul(b[0:EXPERTS, 0:1], table("upto64", EXPERTS), NB16[0:EXPERTS, 0:1],
                          start=True, stop=True).then_inc(bank_filled, 1)
                pe.wait_ge(ends_ready, l + 1)
                b = start(("list", l))
                pe.matmul(b[0:1, 0:BLOCKS_MAX], table("ones", EXPERTS)[:, 0:1], NB16[0:EXPERTS, 256:256 + BLOCKS_MAX],
                          start=True, stop=True)
                pe.matmul(b[0:1, BLOCKS_MAX:BLOCKS_MAX + 1], NB16[0:EXPERTS, 0:1], table("ones", EXPERTS)[:, 0:1],
                          start=True, stop=True).then_inc(bank_filled, 1)
                b = start(("pos", l))
                for g in range(len(full)):
                    o = b[:, g * EXPERTS:(g + 1) * EXPERTS]
                    for g2 in range(g + 1):
                        pe.matmul(o, table("before128" if g2 == g else "ones"),
                                  M16[:, g2 * EXPERTS:(g2 + 1) * EXPERTS], start=g2 == 0, stop=False)
                    mm = pe.matmul(o, NB16[0:EXPERTS, 128:256], table("start64", EXPERTS), start=False, stop=True)
                mm.then_inc(bank_filled, 1)
                S = SLOTS[l]
                sw2 = arrived(("sw2", l))[:, 0:2 * D].rearrange("p (c n) -> p c n", c=2)

                def act_transposed(g):
                    t = full[g]
                    pe.wait_ge(sa_ready, len(FULL[0]) * l + g + 1)
                    b = start(("sT", l, t))
                    for c in (0, 1):
                        mm = pe.transpose(b[:, c * P:(c + 1) * P], SAW[:, t, c * P:(c + 1) * P], ident)
                    mm.then_inc(bank_filled, 1)

                def shared_out(g, h, c):
                    t = full[g]
                    b = start(("sy", l, t, h)) if c == 0 else bank(("sy", l, t, h))
                    mm = pe.matmul(b[:, :], ST[:, g % 2, c, :], sw2[:, c, h * HALF:(h + 1) * HALF],
                                   start=c == 0, stop=c == 1)
                    if c == 1:
                        mm.then_inc(bank_filled, 1)

                for n_ in range(len(full) * TOP_K):
                    N_ = n_ + l * TOP_K * len(FULL[0])
                    pe.wait_ge(onehot, N_ + 1)
                    pe.matmul(O_BANK[0][0:S, 0:BLOCKS_MAX], ONE_S[:, N_ % 2, 0:S], ONE_B[:, N_ % 2, :],
                              start=n_ == 0, stop=n_ == len(full) * TOP_K - 1).then_inc(onehot_used, 1)
                    g, step = divmod(n_ - TOP_K, TOP_K)
                    if n_ < KD:
                        t = full[-1]
                        b = start(("sh", l, t)) if n_ == 0 else bank(("sh", l, t))
                        mm = pe.matmul(b[:, :].rearrange("p (m c) -> p m c", m=2), HT[:, n_, t * P:(t + 1) * P],
                                       sw13[:, :, n_, :], start=n_ == 0, stop=n_ == KD - 1)
                        if n_ == KD - 1:
                            mm.then_inc(bank_filled, 1)
                    elif step == 0:
                        act_transposed(g)
                    elif step == 2:
                        read_out(("sT", l, full[g]))
                        shared_out(g, 0, 0)
                    elif 3 <= step <= 5:
                        shared_out(g, (step - 2) // 2, step % 2)
                act_transposed(len(full) - 1)
                read_out(("sT", l, full[-1]))
                for h in (0, 1):
                    for c in (0, 1):
                        shared_out(len(full) - 1, h, c)

                L, S = loop[l], SLOTS[l]
                read_out(("sy", l, full[-1], 1))
                pe.wait_ge(idx_ready, l + 1)
                pe.sem_inc(L["y_ps"], 8)
                pe.sem_inc(L["xT_ps"], 1)
                pe.wait_ge(zeros_ready, 1)
                pe.wait_ge(list_ready, 2 * (l + 1))
                always, most = turns_of(l)
                blocks = pe.value_load(LIST[0:1, BLOCKS_MAX:BLOCKS_MAX + 1], min_val=EXPERTS, max_val=UNROLL * most)
                turns = pe.snap((blocks + UNROLL - 1) // UNROLL)

                def tokens_T(v):
                    pe.sem_inc(L["started"], 1)
                    for k in range(KD):
                        mm = pe.transpose(XT_PS[k // 4][:, (k % 4) * S:(k % 4 + 1) * S],
                                          XG[0:S, v, k:D:KD], ident[0:S, 0:S])
                    mm.then_inc(L["xT_ps"], 1)

                def act_T():
                    pe.sem_inc(L["started"], 1)
                    pe.transpose(AT_PS[:, 0:S], ACTV[0:S, :], ident[0:S, 0:S]).then_inc(L["actT_ps"], 1)

                def second(u):
                    w2 = expert_w(u)[1]
                    for h in (0, 1):
                        pe.matmul(Y_PS[h][0:S, :], ACTT[:, 0:S], w2[:, h * HALF:(h + 1) * HALF],
                                  start=True, stop=True).then_inc(L["y_ps"], 1)

                def turn(i):
                    for u in range(UNROLL):
                        b = i * UNROLL + u
                        pe.wait_ge(L["act"], b + 1)
                        act_T()
                        pe.wait_ge(L[f"x_in{(u + 1) % UNROLL}"], i * 16 + 16 * ((u + 1) // UNROLL + 1))
                        pe.wait_ge(L["xT_scalar"], b + 1)
                        pe.wait_ge(L["xT_vector"], b + 1)
                        tokens_T((u + 1) % UNROLL)
                        pe.wait_ge(L[f"w_in{u}"], i * 48 + 48)
                        w13 = expert_w(u)[0]
                        for k in range(KD):
                            mm = pe.matmul(AB_PS[0:S, 0:2 * HIDDEN].rearrange("p (m h) -> p m h", m=2),
                                           XGT[:, u % 2, k, 0:S], w13[:, :, k, :], start=k == 0, stop=k == KD - 1)
                        mm.then_inc(L["ab_ps"], 1)
                        pe.wait_ge(L["actT"], b + 1)
                        pe.wait_ge(L["y_scalar"], b + 1)
                        pe.wait_ge(L["y_vector"], b + 1)
                        second((u - 1) % UNROLL)

                pe.wait_ge(L["x_in0"], 16)
                tokens_T(0)
                with pe.Fori(0, always) as i:
                    turn(i)
                with pe.Fori(always, most) as i:
                    with pe.If(i < turns):
                        turn(i)
                total = turns * UNROLL
                pe.wait_ge(L["act"], total + 1)
                pe.wait_ge(L["act"], EXPERTS)
                act_T()
                pe.wait_ge(L["actT"], total + 1)
                pe.wait_ge(L["y_scalar"], total + 1)
                pe.wait_ge(L["y_vector"], total + 1)
                pe.wait_ge(L["y_vector"], EXPERTS)
                second(UNROLL - 1)
                pe.wait_ge(L["xT_scalar"], total + 1)
                pe.wait_ge(L["xT_vector"], total + 1)
                pe.wait_ge(L["y_scalar"], total + 2)
                pe.wait_ge(L["y_vector"], total + 2)
                pe.wait_ge(L["y_vector"], EXPERTS)

        @block.scalar
        def _(act):
            done = [0]
            steps = [0]

            def filled(name):
                act.wait_ge(bank_filled, jobs.filled(name))
                return bank(name)

            def drained(name, ins):
                done[0] += 1
                assert jobs.of[name][1:] == ("scalar", done[0]), name
                ins.then_inc(by_scalar, 1)

            def copy(dst, src, scale=None):
                if scale is None:
                    return nc.scalar.activation(dst, src, ACT.Copy)
                return nc.scalar.activation(dst, src, ACT.Copy, scale=scale)

            act.wait_ge(consts_in, 3 * 16)
            nc.scalar.activation(CS, CS, ACT.Silu).then_inc(silu_c, 1)

            def ada(l, c):
                b = filled(("ada", l, c))
                n = ada_order.index((l, c))
                if n >= 2:
                    act.wait_ge(row_sent[n % 2], 16 * (n // 2))
                drained(("ada", l, c), copy(MROW[:, n % 2, :], b[0:2, :]))

            for l in range(DEPTH):
                for n in (0, 1):
                    act.wait_ge(sin_arg, 2 * l + n + 1)
                    nc.scalar.activation(FH[0:FHID, 2 + n, :], FH[0:FHID, 0, :], ACT.Sin).then_inc(sin_out, 1)
                    if l == 0:
                        for c in ((0,), (1, 2, 3))[n]:
                            ada(0, c)

            for l in range(DEPTH):
                full = FULL[l]
                first = full[0] * P
                for c in range(ADA_EARLY, ADA_LATE if l else 0):
                    ada(l, c)
                for t in range(TILES):
                    b = filled(("hT", l, 1, t, 0))
                    drained(("hT", l, 1, t, 0), copy(HT[:, 0:4, t * P:(t + 1) * P], b[:, :].rearrange("p (k t) -> p k t", k=4)))
                for t in full:
                    b = filled(("q", l, t))
                    drained(("q", l, t), copy(QKV[:, t, 0:512].rearrange("p (c s d) -> p c s d", s=2, c=4),
                                              b[:, :].rearrange("p (s c d) -> p c s d", s=2, c=4)))
                if l == 0:
                    ada(l, ADA_VECTOR[0])
                for t in range(TILES):
                    drained(("kv", l, t), copy(QKV[:, t, 512:1024], filled(("kv", l, t))[:, :]))
                if l == 0:
                    ada(l, ADA_VECTOR[1])
                for f in range(4):
                    b = filled(("bqk", l, f))
                    lo = first if f < 2 else 0
                    drained(("bqk", l, f), copy(BQK[:, f, lo:HALF], b[:, lo:HALF], HEAD ** -0.5 if f < 2 else None))
                if l == 0:
                    ada(l, ADA_VECTOR[2])
                act.wait_ge(pads_ready, l + 1)
                for f in range(6):
                    b = filled(("c", l, f))
                    s0 = full[0] // 2
                    drained(("c", l, f), copy(CP[:, f, s0:2, 1:SEQ + 1],
                                              b[:, first:HALF].rearrange("p (s t) -> p s t", t=SEQ)))
                if l == 0:
                    ada(l, ADA_VECTOR[3])
                for c in range(8, 12 if l == 0 else 0):
                    ada(l, c)
                for t in range(TILES):
                    if t in full:
                        b = filled(("qT", l, t))
                        drained(("qT", l, t), copy(QA[:, :, t * P:(t + 1) * P], b[:, :].rearrange("p (c t) -> p c t", c=4)))
                    b = filled(("kT", l, t))
                    act.wait_ge(qn_ready, TILES * (l + 1))
                    copy(KP[64:P, 0, t, :], b[64:P, 0:P]).then_inc(keys_padded, 1)
                    drained(("kT", l, t), copy(KA0[0:64, t * P:(t + 1) * P], b[0:64, 0:P]))
                for t in full:
                    b = filled(("uT", l, t))
                    drained(("uT", l, t), copy(UT[:, t, :], b[:, 0:C_CH]))
                mine = units[l]
                n = len(mine)
                for i in range(n + S_AHEAD):
                    if i < n:
                        nk = len(mine[i][3]) * P
                        U = unit_base[l] + i
                        b = filled(("S", l, i))
                        act.wait_ge(max_ready, U + 1)
                        if i >= 2:
                            act.wait_ge(bank_filled, jobs.filled(("PT", l, i - 2)))
                        if U >= 4:
                            act.wait_ge(o_read, U - 3)
                        drained(("S", l, i), nc.scalar.activation(
                            PB[:, i % 2, 0:nk], b[:, 0:nk], ACT.Exp, bias=NM[:, U % 4:U % 4 + 1],
                            accum_out=SM[:, U % 4:U % 4 + 1]))
                    u = i - S_AHEAD
                    if u >= 0 and u % 2 == 1:
                        nk = len(mine[u][3]) * P
                        b = filled(("PT", l, u))
                        if u >= 2:
                            act.wait_ge(o_filled, unit_base[l] + u - 1)
                        drained(("PT", l, u), copy(PT[:, u % 2, 0:nk], b[:, 0:nk]))
                for t in full:
                    for h in (0, 1):
                        b = filled(("oT", l, t, h))
                        nch = 2 if h else 4
                        drained(("oT", l, t, h), copy(OT[:, 4 * h:4 * h + nch, t * P:(t + 1) * P],
                                                      b[:, 0:nch * P].rearrange("p (c t) -> p c t", c=nch)))
                for c in AFTER_OUT[l]:
                    ada(1, c)
                base = TILES + (l * (TILES + len(FULL[0])))
                for g, t in enumerate(full):
                    act.wait_ge(h_ready, base + g + 1)
                    act.dma_start(h_dram[t * P:(t + 1) * P, :], HN[:, t, :]).then_inc(h_stored, 16)
                    b = filled(("hT", l, 2, t, 0))
                    drained(("hT", l, 2, t, 0), copy(HT[:, 0:4, t * P:(t + 1) * P], b[:, :].rearrange("p (k t) -> p k t", k=4)))
                b = filled(("rt", l))
                w = EXPERTS * len(full)
                drained(("rt", l), nc.scalar.activation(RT[:, 0, 0:w], b[:, 0:w], ACT.Exp, scale=-1.0))
                for g, t in enumerate(full):
                    n_ = len(FULL[0]) * l + g
                    b = filled(("sh", l, t))
                    if g >= 2:
                        act.wait_ge(sa_ready, n_ - 1)
                    nc.scalar.activation(SG[:, g % 2, :], b[:, 0:SHARED], ACT.Silu).then_inc(sg_ready, 1)
                for g, t in enumerate(full):
                    b = filled(("sT", l, t))
                    drained(("sT", l, t), copy(ST[:, g % 2, :, :], b[:, 0:2 * P].rearrange("p (c t) -> p c t", c=2)))
                    for h in (0, 1):
                        b = filled(("sy", l, t, h))
                        drained(("sy", l, t, h), copy(MACC[:, t, h * HALF:(h + 1) * HALF], b[:, :]))

                L, S = loop[l], SLOTS[l]
                act.sem_inc(L["y_scalar"], 1)
                act.wait_ge(h_stored, 16 * (len(FULL[0]) * l + len(full)))
                act.wait_ge(list_ready, 2 * (l + 1))
                always, most = turns_of(l)
                blocks = act.value_load(LIST[0:1, BLOCKS_MAX:BLOCKS_MAX + 1], min_val=EXPERTS, max_val=UNROLL * most)
                turns = act.snap((blocks + UNROLL - 1) // UNROLL)

                def tokens_T(v):
                    copy(XGT[:, v, 0:4, 0:S], XT_PS[0][:, 0:4 * S].rearrange("p (k t) -> p k t", k=4)).then_inc(L["xT_scalar"], 1)

                def act_T():
                    copy(ACTT[:, 0:S], AT_PS[:, 0:S]).then_inc(L["actT"], 1)

                def second(b, w, turns_):
                    act.wait_ge(L["y_ps"], b * 2 + 9)
                    act.wait_ge(L[f"y_out{w}"], turns_ * 16 + 16)
                    copy(YSB[0:S, w, 0:HALF], Y_PS[0][0:S, :]).then_inc(L["y_scalar"], 1)

                def turn(i):
                    for u in range(UNROLL):
                        b = i * UNROLL + u
                        act.wait_ge(L["actT_ps"], b + 1)
                        act_T()
                        act.wait_ge(L["xT_ps"], b + 3)
                        tokens_T((u + 1) % 2)
                        act.wait_ge(L["ab_ps"], b + 1)
                        nc.scalar.activation(SIL[0:S, :], AB_PS[0:S, 0:HIDDEN], ACT.Silu).then_inc(L["silu"], 1)
                        second(b, (u - 1) % UNROLL, i)

                act.wait_ge(L["xT_ps"], 2)
                tokens_T(0)
                with act.Fori(0, always) as i:
                    turn(i)
                with act.Fori(always, most) as i:
                    with act.If(i < turns):
                        turn(i)
                total = act.snap(turns * UNROLL)
                act.wait_ge(L["actT_ps"], total + 1)
                act.wait_ge(L["actT_ps"], EXPERTS)
                act_T()
                second(total, UNROLL - 1, turns)

        @block.vector
        def _(dve):
            done = [0]
            steps = [0]

            def link(ins):
                steps[0] += 1
                ins.then_inc(vector_step, 1)
                dve.wait_ge(vector_step, steps[0])

            def free(ins):
                steps[0] += 1
                ins.then_inc(vector_step, 1)

            def filled(name):
                dve.wait_ge(bank_filled, jobs.filled(name))
                return bank(name)

            def drained(name, ins):
                done[0] += 1
                assert jobs.of[name][1:] == ("vector", done[0]), name
                ins.then_inc(by_vector, 1)
                dve.wait_ge(by_vector, done[0])

            tt = dve.tensor_tensor
            ts = dve.tensor_scalar
            stt = dve.scalar_tensor_tensor

            def rsqrt(v, n, scale):
                x, y, w = NV[:, 0:n], RS[:, 0:n].bitcast(F32), NT[:, 0:n]
                link(ts(x, v, scale, EPS, ALU.mult, ALU.add))
                link(ts(RS[:, 0:n], x.bitcast(I32), -0.5, float(0x5F3759DF), ALU.mult, ALU.add))
                for _ in range(3):
                    link(tt(w, y, y, ALU.mult))
                    link(stt(w, w, -0.5, x, ALU.mult, ALU.mult))
                    link(stt(y, w, 1.5, y, ALU.add, ALU.mult))

            def normalise(tiles, out_):
                for t in tiles:
                    for h in (0, 1):
                        free(dve.bn_stats(out=STAT[:, t, 6 * h:6 * h + 6], in_=X[:, t, h * HALF:(h + 1) * HALF]))
                dve.wait_ge(vector_step, steps[0])
                for t in tiles:
                    free(dve.bn_aggr(out=MV[:, t, :], in_=STAT[:, t, :]))
                dve.wait_ge(vector_step, steps[0])
                rsqrt(MV[:, tiles[0]:tiles[-1] + 1, 1], len(tiles), 1.0)
                for g, t in enumerate(tiles):
                    free(ts(out_[:, t, :], X[:, t, :], MV[:, t, 0:1], RS[:, g:g + 1].bitcast(F32),
                            ALU.subtract, ALU.mult))
                dve.wait_ge(vector_step, steps[0])

            dve.wait_ge(consts_in, 3 * 16)
            dve.wait_ge(once_in, 7 * 16)
            dve.tensor_copy(TRI[:, :], ONCE_SB).then_inc(tables_ready, 1)
            for l in range(DEPTH):
                for n, name in enumerate((("fil1", l), ("fil2", l))):
                    b = filled(name)
                    arg, turns_ = FH[0:FHID, 0, :], FH[0:FHID, 1, :]
                    if l + n:
                        dve.wait_ge(sin_out, 2 * l + n)
                    drained(name, ts(arg, b[0:FHID, 0:SEQ], FCOL[:, l, 2 * n:2 * n + 1], FCOL[:, l, 2 * n + 1:2 * n + 2],
                                     ALU.add, ALU.mult))
                    link(ts(turns_, arg, 1.0 / (2 * math.pi), 12582912.0, ALU.mult, ALU.add))
                    link(ts(turns_, turns_, 12582912.0, None, ALU.subtract))
                    link(stt(arg, turns_, -6.28125, arg, ALU.mult, ALU.add))
                    link(stt(arg, turns_, -(2 * math.pi - 6.28125), arg, ALU.mult, ALU.add))
                    ts(arg, arg, 3.1415925, -3.1415925, ALU.min, ALU.max).then_inc(sin_arg, 1)
                for t in (0, 1):
                    b = filled(("fil3", l, t))
                    drained(("fil3", l, t), tt(FT[:, t, :], b[:, :], DECAY[:, t, :], ALU.mult))
                if l:
                    dve.wait_ge(bank_filled, jobs.filled(("filK", l - 1, 1, 1)))
                for t in (0, 1):
                    free(tt(FS[:, t, 0:C_CH], FT[:, t, 0:C_CH], FT[:, t, C_CH:2 * C_CH], ALU.add))
                    free(tt(FS[:, t, C_CH:2 * C_CH], FT[:, t, 0:C_CH], FT[:, t, C_CH:2 * C_CH], ALU.subtract))
                dve.wait_ge(vector_step, steps[0])
                dve.nop().then_inc(filt_ready, 1)
                if l == 0:
                    dve.wait_ge(x_in, 4 * 16)
                    normalise(tuple(range(TILES)), HN)
                for m in (0, 1):
                    for cs in (0, 1):
                        b = filled(("filK", l, m, cs))
                        drained(("filK", l, m, cs), dve.tensor_copy(KF[:, l, m, cs, :], b[:, 0:C_CH]))
            link(dve.memset(KA0[64:P, :], 0.0))
            dve.memset(ACTV[:, :], 0.0).then_inc(zeros_ready, 1)
            dve.wait_ge(small_in, 3 * 16)
            link(ts(GAIN[:, :, 0, :], GAIN[:, :, 0, :], HEAD ** -0.5, None, ALU.mult))

            for l in range(DEPTH):
                full = FULL[l]
                ns = len(full) // 2
                lo = full[0] * P

                batches = [full[i:i + len(full) // 2] for i in (0, len(full) // 2)]

                def modulate(which, tiles):
                    dve.wait_ge(moda_in, 64 * (2 * l + which))
                    for t in tiles:
                        link(stt(HN[:, t, :], MODA[:, 1, t // 2, :], 1.0, HN[:, t, :], ALU.add, ALU.mult))
                        tt(HN[:, t, :], HN[:, t, :], MODA[:, 0, t // 2, :], ALU.add).then_inc(h_ready, 1)

                def transposed(which, tiles):
                    for t in tiles:
                        b = filled(("hT", l, which, t, 1))
                        drained(("hT", l, which, t, 1), dve.tensor_copy(
                            HT[:, 4:8, t * P:(t + 1) * P], b[:, :].rearrange("p (k t) -> p k t", k=4)))
                    dve.nop().then_inc(moda_used, 1)

                def post_norm(which, tiles):
                    normalise(tiles, X)
                    dve.wait_ge(norm_in, 32 * (2 * l + which))
                    for t in tiles:
                        link(tt(X[:, t, :], X[:, t, :], LNB[:, 0, :], ALU.mult))
                        link(tt(X[:, t, :], X[:, t, :], LNB[:, 1, :], ALU.add))

                modulate(1, tuple(range(TILES)))
                transposed(1, tuple(range(TILES)))
                for e in (0, SEQ + 1):
                    free(dve.memset(CP[:, :, :, e:e + 1], 0.0))
                dve.wait_ge(vector_step, steps[0])
                dve.nop().then_inc(pads_ready, 1)

                def summed(n):
                    it = ("ada", 0, ADA_VECTOR[n])
                    at = item_at[it]
                    dve.wait_ge(ring_in[at % RING], ring_arrivals(at))
                    if n >= 2:
                        dve.wait_ge(bank_filled, jobs.filled(("ada", 0, ADA_VECTOR[n - 2])))
                    w = item(it).rearrange("p (k c) -> p k c", k=KD)
                    for k in range(KD):
                        for v in (0, 1):
                            if k == 0:
                                free(ts(ACC[n % 2][:, v, :], w[:, k, :], CS[:, k, v:v + 1], None, ALU.mult))
                            else:
                                free(stt(ACC[n % 2][:, v, :], w[:, k, :], CS[:, k, v:v + 1], ACC[n % 2][:, v, :],
                                         ALU.mult, ALU.add))
                        dve.wait_ge(vector_step, steps[0])
                    dve.nop().then_inc(partial_sums, 1)

                if l == 0:
                    dve.wait_ge(silu_c, 1)
                    summed(0)
                    summed(1)
                    summed(2)
                    dve.wait_ge(bank_filled, jobs.filled(("ada", 0, ADA_VECTOR[1])))

                dve.wait_ge(by_scalar, jobs.of[("kv", l, TILES - 1)][2])
                for t in range(TILES):
                    h0 = 0 if t in full else 8
                    src = QKV[:, t, 0:640].rearrange("p (h d) -> p h d", h=10)[:, h0:10, :]
                    link(tt(SQ[:, h0:10, :], src, src, ALU.mult))
                    link(dve.tensor_reduce(SS[:, 10 * t + h0:10 * t + 10], SQ[:, h0:10, :], AX.X, ALU.add))
                    if h0:
                        free(dve.memset(SS[:, 10 * t:10 * t + h0], 1.0))
                dve.wait_ge(vector_step, steps[0])
                rsqrt(SS[:, :], 40, 1.0 / HEAD)
                for t in range(TILES):
                    h0 = 0 if t in full else 8
                    n = 10 - h0
                    src = QKV[:, t, 0:640].rearrange("p (h d) -> p h d", h=10)
                    rs = RS[:, 10 * t + h0:10 * t + 10].bitcast(F32).unsqueeze(2).to_broadcast([P, n, HEAD])
                    link(tt(SQ[:, h0:10, :], src[:, h0:10, :], rs, ALU.mult))
                    dst = SQ if t >= 2 else QN[:, t]
                    if not h0:
                        free(tt(dst[:, 0:8, :], SQ[:, 0:8, :], GAIN[:, l, 0, :].unsqueeze(1).to_broadcast([P, 8, HEAD]), ALU.mult))
                    g = tt(dst[:, 8:10, :], SQ[:, 8:10, :], GAIN[:, l, 1, :].unsqueeze(1).to_broadcast([P, 2, HEAD]), ALU.mult)
                    if t < 2:
                        link(g)
                        dve.nop().then_inc(qn_ready, 1)
                        continue
                    link(g)
                    c = const("cos")[:, 32 * (t - 2):32 * (t - 1)].unsqueeze(1).to_broadcast([P, 10, 32])
                    s = const("sin")[:, 32 * (t - 2):32 * (t - 1)].unsqueeze(1).to_broadcast([P, 10, 32])
                    x1, x2 = SQ[:, :, 0:HEAD:2], SQ[:, :, 1:HEAD:2]
                    free(tt(RP[:, 0], x1, c, ALU.mult))
                    free(tt(RP[:, 1], x2, s, ALU.mult))
                    dve.wait_ge(vector_step, steps[0])
                    link(tt(QN[:, t, :, 0:HEAD:2], RP[:, 0], RP[:, 1], ALU.subtract))
                    free(tt(RP[:, 0], x1, s, ALU.mult))
                    free(tt(RP[:, 1], x2, c, ALU.mult))
                    dve.wait_ge(vector_step, steps[0])
                    tt(QN[:, t, :, 1:HEAD:2], RP[:, 0], RP[:, 1], ALU.add).then_inc(qn_ready, 1)
                    dve.wait_ge(qn_ready, TILES * l + t + 1)

                if l == 0:
                    summed(3)

                dve.wait_ge(by_scalar, jobs.of[("c", l, 5)][2])
                s0 = 2 - ns
                for f in range(6):
                    def w(i):
                        return HYC[:, l, 3 * f + i:3 * f + i + 1]
                    z = OT[:, f, lo:HALF].rearrange("p (s t) -> p s t", t=SEQ)
                    link(ts(z, CP[:, f, s0:2, 0:SEQ], w(0), HYC[:, l, 18 + f:19 + f], ALU.mult, ALU.add))
                    link(stt(z, CP[:, f, s0:2, 1:SEQ + 1], w(1), z, ALU.mult, ALU.add))
                    link(stt(z, CP[:, f, s0:2, 2:SEQ + 2], w(2), z, ALU.mult, ALU.add))
                link(tt(OT[:, 2:4, lo:HALF], OT[:, 2:4, lo:HALF], OT[:, 4:6, lo:HALF], ALU.mult))
                dve.nop().then_inc(u_ready, 1)
                T1, T2 = PT[:, 0, 0:ns * C_CH], PT[:, 1, 0:ns * C_CH]
                T1, T2 = (x.rearrange("p (s c) -> p s c", s=ns) for x in (T1, T2))
                for m in (0, 1):
                    kc, ks = (KF[:, l, m, cs, :].unsqueeze(1).to_broadcast([P, ns, C_CH]) for cs in (0, 1))
                    yc, ys = (YF[:, m, cs, 0:ns * C_CH].rearrange("p (s c) -> p s c", s=ns) for cs in (0, 1))
                    b = filled(("U", l, m, 0))[:, 0:ns * C_CH].rearrange("p (s c) -> p s c", s=ns)
                    link(tt(yc, b, kc, ALU.mult))
                    drained(("U", l, m, 0), tt(ys, b, ks, ALU.mult))
                    b = filled(("U", l, m, 1))[:, 0:ns * C_CH].rearrange("p (s c) -> p s c", s=ns)
                    link(tt(T1, b, ks, ALU.mult))
                    drained(("U", l, m, 1), tt(T2, b, kc, ALU.mult))
                    link(tt(yc, yc, T1, ALU.subtract))
                    tt(ys, ys, T2, ALU.add).then_inc(yf_ready, 1)
                    dve.wait_ge(yf_ready, 2 * l + m + 1)
                for ct in (0, 1):
                    b = filled(("yh", l, ct))
                    t1 = PT[:, 0, 0:ns * SEQ]
                    link(stt(t1, OT[:, 2 + ct, lo:HALF], HYC[:, l, 24 + ct:25 + ct], b[:, 0:ns * SEQ], ALU.mult, ALU.add))
                    drained(("yh", l, ct), tt(OT[:, 6 + ct, lo:HALF], t1, OT[:, ct, lo:HALF], ALU.mult))

                n = item_at[("mixc", l)]
                dve.wait_ge(ring_in[n % RING], ring_arrivals(n))
                bias = item(("mixc", l))[:, 8 * SEQ:16 * SEQ].rearrange("p (t h c) -> p t h c", t=2, h=B_HEADS)
                dve.wait_ge(mask_in, 16 * (l + 1))
                mask = MASK_SB
                for t in (0, 1):
                    for h2 in (0, 2):
                        link(tt(bias[:, t, h2:h2 + 2, :], bias[:, t, h2:h2 + 2, :],
                                mask[:, t, :].unsqueeze(1).to_broadcast([P, 2, SEQ]), ALU.add))
                mine = units[l]
                n = len(mine)
                for i in range(n + S_AHEAD + PV_LAG):
                    if i < n:
                        t, kind, h, keys = mine[i]
                        nk = len(keys) * P
                        U = unit_base[l] + i
                        b = filled(("S", l, i))
                        if kind == "B" and t >= 2:
                            link(tt(b[:, 2 * P:4 * P], b[:, 2 * P:4 * P], bias[:, t - 2, h, :], ALU.add))
                        if i >= 4:
                            dve.wait_ge(by_scalar, jobs.of[("S", l, i - 4)][2])
                        dve.tensor_reduce(NM[:, U % 4:U % 4 + 1], b[:, 0:nk], AX.X, ALU.max, negate=True).then_inc(max_ready, 1)
                    u = i - S_AHEAD
                    if 0 <= u < n and u % 2 == 0:
                        nk = len(mine[u][3]) * P
                        b = filled(("PT", l, u))
                        if u >= 2:
                            dve.wait_ge(o_filled, unit_base[l] + u - 1)
                        drained(("PT", l, u), dve.tensor_copy(PT[:, u % 2, 0:nk], b[:, 0:nk]))
                    u = i - S_AHEAD - PV_LAG
                    if 0 <= u < n:
                        t, kind, h, keys = mine[u]
                        U = unit_base[l] + u
                        dve.wait_ge(by_scalar, jobs.of[("S", l, u)][2])
                        link(dve.reciprocal(RC[:, U % 4:U % 4 + 1], SM[:, U % 4:U % 4 + 1]))
                        dve.wait_ge(o_filled, U + 1)
                        col = 64 * (2 * (h % 4) + h // 4) if kind == "A" else 512 + 64 * h
                        ts(OTOK[:, t, col:col + 64], O_BANK[U % 2][:, 0:HEAD],
                           RC[:, U % 4:U % 4 + 1], None, ALU.mult).then_inc(o_read, 1)
                dve.nop().then_inc(bias_used, 1)

                dve.wait_ge(modg_in, 32 * (2 * l + 1))
                for batch in batches:
                    for t in batch:
                        for h in (0, 1):
                            cols = slice(h * HALF, (h + 1) * HALF)
                            b = filled(("wo", l, t, h))
                            tmp = PB[:, h, :]
                            drained(("wo", l, t, h), tt(tmp, b[:, :], MODG[:, t // 2, cols], ALU.mult))
                            link(stt(X[:, t, cols], X[:, t, cols], ALPHA, tmp, ALU.mult, ALU.add))
                    post_norm(1, batch)
                    normalise(batch, HN)
                    modulate(2, batch)
                dve.nop().then_inc(modg_used, 1)
                dve.nop().then_inc(norm_used, 1)
                transposed(2, full)

                W_ = EXPERTS * len(full)
                nt = len(full)

                def R(i, w=W_):
                    return RT[:, i, 0:w]

                def R3(i):
                    return R(i).rearrange("p (t e) -> p t e", t=nt)
                dve.wait_ge(by_scalar, jobs.of[("rt", l)][2])
                link(ts(R(0), R(0), 1.0, None, ALU.add))
                link(dve.reciprocal(R(0), R(0)))
                link(tt(R3(1), R3(0), RB[:, l, :].unsqueeze(1).to_broadcast([P, nt, EXPERTS]), ALU.add))
                G = nt * GROUPS
                sel8 = R(1).rearrange("p (g e) -> p g e", e=8)
                hi4, lo4 = (RT[:, 2, o:o + 4 * G].rearrange("p (g e) -> p g e", e=4) for o in (0, 128))
                hi2, lo2, m2 = (RT[:, 3, o:o + 2 * G].rearrange("p (g e) -> p g e", e=2) for o in (0, 64, 128))
                hi1, lo1, m1 = (RT[:, 4, o:o + G].rearrange("p (g e) -> p g e", e=1) for o in (0, 32, 64))
                free(tt(hi4, sel8[:, :, 0:4], sel8[:, :, 4:8], ALU.max))
                link(tt(lo4, sel8[:, :, 0:4], sel8[:, :, 4:8], ALU.min))
                for (hi, lo_), (hi_, lo__, mid), w in (((hi4, lo4), (hi2, lo2, m2), 2), ((hi2, lo2), (hi1, lo1, m1), 1)):
                    free(tt(hi_, hi[:, :, 0:w], hi[:, :, w:2 * w], ALU.max))
                    free(tt(mid, hi[:, :, 0:w], hi[:, :, w:2 * w], ALU.min))
                    link(tt(lo__, lo_[:, :, 0:w], lo_[:, :, w:2 * w], ALU.max))
                    link(tt(lo__, lo__, mid, ALU.max))
                gs = RT[:, 4, 96:96 + G].rearrange("p (t g) -> p t g", t=nt)
                link(tt(gs.rearrange("p t g -> p (t g)"), hi1.rearrange("p g e -> p (g e)"), lo1.rearrange("p g e -> p (g e)"), ALU.add))
                mine_ = gs.unsqueeze(3).to_broadcast([P, nt, 8, 8])
                others = gs.unsqueeze(2).to_broadcast([P, nt, 8, 8])
                gt = R(2).rearrange("p (t g h) -> p t g h", t=nt, g=8)
                eq = R(3).rearrange("p (t g h) -> p t g h", t=nt, g=8)
                before = const("before8").rearrange("p (g h) -> p g h", g=8).unsqueeze(1).to_broadcast([P, nt, 8, 8])
                link(tt(gt, others, mine_, ALU.is_gt))
                link(tt(eq, others, mine_, ALU.is_equal))
                link(tt(eq, eq, before, ALU.mult))
                link(tt(R(2), R(2), R(3), ALU.add))
                rank = RT[:, 4, 0:G]
                link(dve.tensor_reduce(rank, R(2).rearrange("p (g h) -> p g h", h=8), AX.X, ALU.add))
                link(ts(rank, rank, TOP_GROUPS - 0.5, MASKED, ALU.is_gt, ALU.mult))
                link(tt(R(1).rearrange("p (g e) -> p g e", e=8), sel8, rank.unsqueeze(2).to_broadcast([P, G, 8]), ALU.add))
                for g in range(nt):
                    free(dve.max(out=P8[:, g, :], in_=R3(1)[:, g, :]))
                dve.wait_ge(vector_step, steps[0])
                for g in range(nt):
                    free(dve.match_replace(out=R3(2)[:, g, :], in_to_replace=P8[:, g, :], in_values=R3(1)[:, g, :],
                                           imm_value=-3e38))
                dve.wait_ge(vector_step, steps[0])
                M16 = RT[:, 10, :].bitcast(BF16)[:, 0:W_]
                link(tt(R(3), R(2), R(1), ALU.not_equal))
                dve.tensor_copy(M16, R(3)).then_inc(mask_ready, 1)
                dve.wait_ge(mask_ready, l + 1)
                link(tt(R(0), R(0), R(3), ALU.mult))
                ws = NT[:, 0:nt]
                link(dve.tensor_reduce(ws, R3(0), AX.X, ALU.add))
                link(dve.reciprocal(ws, ws))
                link(ts(ws, ws, ROUTED_SCALE, None, ALU.mult))
                link(tt(R3(0), R3(0), ws.unsqueeze(2).to_broadcast([P, nt, EXPERTS]), ALU.mult))

                def shared_act(g, t):
                    n_ = len(FULL[0]) * l + g
                    b = filled(("sh", l, t))
                    dve.wait_ge(sg_ready, n_ + 1)
                    drained(("sh", l, t), tt(SAW[:, t, 0:SHARED], SG[:, g % 2, :], b[:, SHARED:2 * SHARED], ALU.mult))
                    dve.nop().then_inc(sa_ready, 1)

                for g in range(nt - 1):
                    shared_act(g, full[g])
                NB16 = RT[:, 11, :].bitcast(BF16)
                b = filled(("count", l))
                drained(("count", l), dve.tensor_copy(NB1[0:EXPERTS, 0:1], b[0:EXPERTS, 0:1]))
                S = SLOTS[l]
                link(ts(NB1[0:EXPERTS, 1:2], NB1[0:EXPERTS, 0:1], S + 0.5, 1.0, ALU.is_gt, ALU.add))
                for j in range(2, -(-P * nt // S)):
                    link(stt(NB1[0:EXPERTS, 1:2], NB1[0:EXPERTS, 0:1], j * S + 0.5, NB1[0:EXPERTS, 1:2], ALU.is_gt, ALU.add))
                link(dve.tensor_copy(NB16[0:EXPERTS, 0:1], NB1[0:EXPERTS, 1:2]))
                ts(NB16[0:EXPERTS, 128:256], table("ones", EXPERTS), NB1[0:EXPERTS, 1:2], float(S), ALU.mult, ALU.mult).then_inc(nb_ready, 1)
                b = filled(("ends", l))
                drained(("ends", l), dve.tensor_copy(NB1[0:EXPERTS, 2:3], b[0:EXPERTS, 0:1]))
                ts(NB16[0:EXPERTS, 256:256 + BLOCKS_MAX], const("iota_block")[0:EXPERTS, :], NB1[0:EXPERTS, 2:3], None,
                   ALU.is_ge).then_inc(ends_ready, 1)
                b = filled(("list", l))
                ts(LIST[0:1, 0:BLOCKS_MAX], b[0:1, 0:BLOCKS_MAX], float(EXPERTS - 1), None, ALU.min).then_inc(list_ready, 1)
                drained(("list", l), dve.tensor_copy(LIST[0:1, BLOCKS_MAX:BLOCKS_MAX + 1], b[0:1, BLOCKS_MAX:BLOCKS_MAX + 1]))
                dve.nop().then_inc(list_ready, 1)
                b = filled(("pos", l))
                drained(("pos", l), stt(R(5), b[:, 0:W_], 1.0, R(3), ALU.add, ALU.mult))
                for g in range(nt):
                    free(dve.max(out=P8[:, g, :], in_=R3(5)[:, g, :]))
                dve.wait_ge(vector_step, steps[0])
                p8 = P8[:, 0:nt, :].rearrange("p t j -> p (t j)")
                n8 = nt * TOP_K
                slot_i, block_i = PSB[:, 0, 0:n8], PSB[:, 1, 0:n8]
                slot_f, block_f = PSB[:, 2, 0:n8].bitcast(F32), PSB[:, 3, 0:n8].bitcast(F32)
                link(ts(slot_i, p8, 1.0, None, ALU.subtract))
                link(ts(block_i, slot_i, int(math.log2(S)), None, ALU.logical_shift_right))
                link(ts(slot_i, slot_i, S - 1, None, ALU.bitwise_and))
                link(dve.tensor_copy(slot_f, slot_i))
                link(dve.tensor_copy(block_f, block_i))
                for n_ in range(n8):
                    N_ = n_ + l * TOP_K * len(FULL[0])
                    c = full[n_ // TOP_K] * TOP_K + n_ % TOP_K
                    if n_ >= 2:
                        dve.wait_ge(onehot_used, N_ - 1)
                    free(ts(ONE_S[:, N_ % 2, :], const("iota_slot"), slot_f[:, n_:n_ + 1], None, ALU.is_equal))
                    ts(ONE_B[:, N_ % 2, :], const("iota_block"), block_f[:, n_:n_ + 1],
                       const("choice")[:, c:c + 1], ALU.is_equal, ALU.mult).then_inc(onehot, 1)
                    dve.wait_ge(vector_step, steps[0])
                    if n_ == KD + 3:
                        shared_act(nt - 1, full[-1])
                dve.wait_ge(onehot_used, TOP_K * (len(FULL[0]) * l + nt))
                b = O_BANK[0]
                link(ts(SPARE[0:S], b[0:S, 0:BLOCKS_MAX], 0.5, float(EMPTY), ALU.is_lt, ALU.mult))
                link(stt(CHOICE[0:S, 1:BLOCKS_MAX + 1], b[0:S, 0:BLOCKS_MAX], -1.0, SPARE[0:S], ALU.add, ALU.add))
                link(dve.tensor_copy(CHOICE[:, 0:1], CHOICE[:, BLOCKS_MAX:BLOCKS_MAX + 1]))
                link(ts(TOKEN[:, :], CHOICE[:, 1:BLOCKS_MAX + 1], int(math.log2(TOP_K)), None, ALU.logical_shift_right))
                dve.nop().then_inc(idx_ready, 1)

                L, S = loop[l], SLOTS[l]
                dve.sem_inc(L["act"], 1)
                dve.sem_inc(L["y_vector"], 1)
                dve.wait_ge(h_stored, 16 * (len(FULL[0]) * l + nt))
                always, most = turns_of(l)
                blocks = dve.value_load(LIST[0:1, BLOCKS_MAX:BLOCKS_MAX + 1], min_val=EXPERTS, max_val=UNROLL * most)
                turns = dve.snap((blocks + UNROLL - 1) // UNROLL)

                def tokens_T(v):
                    dve.tensor_copy(XGT[:, v, 4:8, 0:S], XT_PS[1][:, 0:4 * S].rearrange("p (k t) -> p k t", k=4)).then_inc(L["xT_vector"], 1)

                def second(b, w, turns_):
                    dve.wait_ge(L["y_ps"], b * 2 + 10)
                    dve.wait_ge(L[f"y_out{w}"], turns_ * 16 + 16)
                    dve.tensor_copy(YSB[0:S, w, HALF:D], Y_PS[1][0:S, :]).then_inc(L["y_vector"], 1)

                def turn(i):
                    for u in range(UNROLL):
                        b = i * UNROLL + u
                        dve.wait_ge(L["xT_ps"], b + 3)
                        tokens_T((u + 1) % 2)
                        dve.wait_ge(L["silu"], b + 1)
                        tt(ACTV[0:S, :], SIL[0:S, :], AB_PS[0:S, HIDDEN:2 * HIDDEN], ALU.mult).then_inc(L["act"], 1)
                        second(b, (u - 1) % UNROLL, i)

                dve.wait_ge(L["xT_ps"], 2)
                tokens_T(0)
                with dve.Fori(0, always) as i:
                    turn(i)
                with dve.Fori(always, most) as i:
                    with dve.If(i < turns):
                        turn(i)
                second(dve.snap(turns * UNROLL), UNROLL - 1, turns)

                for g in range(nt):
                    for j in range(TOP_K):
                        free(stt(RT[:, 6, 0:EXPERTS], R3(5)[:, g, :], P8[:, g, j:j + 1], R3(0)[:, g, :], ALU.is_equal, ALU.mult,
                                 accum_out=G8[:, g, j:j + 1]))
                        dve.wait_ge(vector_step, steps[0])
                dve.wait_ge(by_scalar, jobs.of[("sy", l, full[-1], 1)][2])
                base = l * len(FULL[0]) * TOP_K // 2
                for batch in batches:
                    for t in batch:
                        g = full.index(t)
                        for j in range(0, TOP_K, 2):
                            N_ = base + (g * TOP_K + j) // 2
                            dve.wait_ge(gathered[N_ % 4], 16 * (N_ // 4 + 1))
                            link(stt(MACC[:, t, :], YG[N_ % 4][:, 0, :], G8[:, g, j:j + 1], MACC[:, t, :],
                                     ALU.mult, ALU.add))
                            stt(MACC[:, t, :], YG[N_ % 4][:, 1, :], G8[:, g, j + 1:j + 2], MACC[:, t, :],
                                ALU.mult, ALU.add).then_inc(choice_used, 1)
                            dve.wait_ge(choice_used, N_ + 1)
                        dve.wait_ge(modg_in, 32 * (2 * l + 2))
                        link(tt(MACC[:, t, :], MACC[:, t, :], MODG[:, t // 2, :], ALU.mult))
                        link(stt(X[:, t, :], X[:, t, :], ALPHA, MACC[:, t, :], ALU.mult, ALU.add))
                    post_norm(2, batch)
                    if l < DEPTH - 1:
                        normalise(batch, HN)
                    else:
                        for t in batch:
                            dve.nop().then_inc(out_ready, 1)
                dve.nop().then_inc(modg_used, 1)
                dve.nop().then_inc(norm_used, 1)

        @block.gpsimd
        def _(pool):
            def load(dst, src, s):
                pool.dma_start(dst, src).then_inc(s, 16)

            def row(src):
                return src.partition_broadcast(P)

            for l in range(DEPTH):
                for v in (0, 1):
                    load(mod_dram[l, v:v + 1, :], a["ada_b"][l:l + 1, :], bias_rows)
            pool.wait_ge(bias_rows, 64)
            load(GAIN[:, :, 0, :], a["q_gain"].partition_broadcast(P), small_in)
            load(GAIN[:, :, 1, :], a["k_gain"].partition_broadcast(P), small_in)
            load(RB, a["router_b"].partition_broadcast(P), small_in)

            def send(l, c):
                n = ada_order.index((l, c))
                pool.wait_ge(by_scalar, jobs.of[("ada", l, c)][2])
                pool.dma_start(mod_dram[l, :, c * HALF:(c + 1) * HALF], MROW[:, n % 2, :],
                               accum_op=ALU.add).then_inc(row_sent[n % 2], 16)

            def sent(l, c):
                n = ada_order.index((l, c))
                pool.wait_ge(row_sent[0], 16 * (n // 2 + 1))
                pool.wait_ge(row_sent[1], 16 * ((n + 1) // 2))

            def part(l, i, v):
                return mod_dram[l, v, i * D:(i + 1) * D].partition_broadcast(P)

            def shift_scale(l, which):
                for w in (0, 1):
                    for v in (0, 1):
                        load(MODA[:, w, v, :], part(l, 3 * (which - 1) + w, v), moda_in)

            def gates(l, which):
                for v in (0, 1):
                    load(MODG[:, v, :], part(l, 3 * which - 1, v), modg_in)

            def norm_rows(l, which):
                load(LNB[:, 0, :], a[f"ln{which}_g"][l].partition_broadcast(P), norm_in)
                load(LNB[:, 1, :], a[f"ln{which}_b"][l].partition_broadcast(P), norm_in)

            for l in range(DEPTH):
                full = FULL[l]
                nt = len(full)
                for c in range(ADA_EARLY if l else 0, 4):
                    send(l, c)
                sent(l, 3)
                shift_scale(l, 1)
                if l == 0:
                    norm_rows(l, 1)
                    pool.wait_ge(moda_used, 2 * l + 1)
                    load(MASK_SB, a["mask"], mask_in)
                upto = ADA_LATE if l else 12
                for c in range(4, upto):
                    send(l, c)
                sent(l, upto - 1)
                if l:
                    pool.wait_ge(norm_used, 2 * l)
                    norm_rows(l, 1)
                    pool.wait_ge(modg_used, 2 * l)
                gates(l, 1)
                if l:
                    pool.wait_ge(moda_used, 2 * l + 1)
                    load(MASK_SB, a["mask"], mask_in)
                shift_scale(l, 2)
                pool.wait_ge(by_scalar, jobs.of[("bqk", l, 3)][2])
                pool.wait_ge(qn_ready, TILES * (l + 1))
                pool.memset(KP[0:64, 0], 0.0).then_inc(keys_padded, 1)
                for h in range(B_HEADS):
                    rows = slice(64 * (h % 2), 64 * (h % 2) + 64)
                    other = slice(64 - 64 * (h % 2), P - 64 * (h % 2))
                    pool.memset(KP[other, 1 + h], 0.0).then_inc(keys_padded, 1)
                    pool.tensor_copy(KP[rows, 1 + h], BQK[rows, 2 + h // 2, :].rearrange(
                        "p (t c) -> p t c", c=P)).then_inc(keys_padded, 1)
                for c in AFTER_OUT[l]:
                    send(1, c)
                if l:
                    sent(l, 11)
                pool.wait_ge(norm_used, 2 * l + 1)
                norm_rows(l, 2)
                pool.wait_ge(modg_used, 2 * l + 1)
                gates(l, 2)

                L, S = loop[l], SLOTS[l]
                pool.wait_ge(idx_ready, l + 1)
                pool.wait_ge(h_stored, 16 * (len(FULL[0]) * l + nt))
                pool.wait_ge(list_ready, 2 * (l + 1))
                always, most = turns_of(l)
                blocks = pool.value_load(LIST[0:1, BLOCKS_MAX:BLOCKS_MAX + 1], min_val=EXPERTS, max_val=UNROLL * most)
                turns = pool.snap((blocks + UNROLL - 1) // UNROLL)

                def gather(b, v, copies):
                    pool.tensor_copy(IDXB[0:S, v:v + 1], TOKEN[0:S, bass.ds(b, 1)]).then_inc(L["indices_copied"], 1)
                    pool.wait_ge(L["indices_copied"], copies)
                    pool.sem_inc(L["moves"], 1)
                    nc.gpsimd.indirect_dma_start(
                        out=XG[0:S, v, :], out_offset=None, in_=h_dram,
                        in_offset=bass.IndirectOffsetOnAxis(ap=IDXB[0:S, v:v + 1].bitcast(U32), axis=0),
                        bounds_check=TILES * P - 1, oob_is_err=False).then_inc(L[f"x_in{v}"], 16)

                def scatter(b, w, copies, first=False):
                    if not first:
                        pool.wait_ge(L["y_scalar"], b + 2)
                        pool.wait_ge(L["y_vector"], b + 2)
                    pool.tensor_copy(IDYB[0:S, w:w + 1], CHOICE[0:S, bass.ds(b, 1)]).then_inc(L["indices_copied"], 1)
                    pool.wait_ge(L["indices_copied"], copies)
                    pool.sem_inc(L["moves"], 1)
                    nc.gpsimd.indirect_dma_start(
                        out=y_dram, out_offset=bass.IndirectOffsetOnAxis(ap=IDYB[0:S, w:w + 1].bitcast(U32), axis=0),
                        in_=YSB[0:S, w, :], in_offset=None,
                        bounds_check=TILES * P * TOP_K - 1, oob_is_err=False).then_inc(L[f"y_out{w}"], 16)

                def turn(i):
                    for u in range(UNROLL):
                        b = i * UNROLL + u
                        pool.wait_ge(L["xT_ps"], b + 1)
                        gather(b + AHEAD, (u + AHEAD) % UNROLL, b * 2 + AHEAD + UNROLL + 1)
                        scatter(b, (u - 1) % UNROLL, b * 2 + AHEAD + UNROLL + 2)

                pool.wait_ge(moda_used, 2 * l + 2)
                for b in range(AHEAD):
                    gather(b, b, b + 1)
                for w in range(UNROLL):
                    scatter(0, w, AHEAD + w + 1, first=True)
                with pool.Fori(0, always) as i:
                    turn(i)
                with pool.Fori(always, most) as i:
                    with pool.If(i < turns):
                        turn(i)
                scatter(pool.snap(turns * UNROLL), UNROLL - 1, turns * (2 * UNROLL) + AHEAD + UNROLL + 1)
                for w in range(UNROLL):
                    pool.wait_ge(L[f"y_out{w}"], turns * 16 + (32 if w == UNROLL - 1 else 16))
                    pool.wait_ge(L[f"x_in{w}"], turns * 16 + (16 if w < AHEAD else 0))
                pool.wait_ge(L["y_ps"], turns * (2 * UNROLL) + 10)
                pool.wait_ge(L["xT_scalar"], turns * UNROLL + 1)
                pool.wait_ge(L["xT_vector"], turns * UNROLL + 1)
                pool.nop().then_inc(y_sent, 1)


def kernel(**inputs):
    import concourse.bacc as bacc
    from concourse.bass_utils import run_bass_kernel_spmd

    x = {k: np.asarray(v) for k, v in inputs.items()}
    L = DEPTH

    def columns(v, n):
        return np.moveaxis(v.reshape(v.shape[:-1] + (n, P)), -1, 0)

    arrays = dict(constants())
    arrays["x"], arrays["ctx"] = x["x"][0], x["ctx"][0]
    arrays["cond"] = np.stack([x["c_ctx"], x["c"][0]], -1).reshape(P, KD, 2)
    taps = columns(x["hy_conv_w"].transpose(0, 1, 2), 6)
    arrays["hyc"] = np.concatenate([taps.transpose(0, 1, 3, 2).reshape(P, L, 18), columns(x["hy_conv_b"], 6),
                                    columns(x["hy_skip"], 2)], -1)
    arrays["f_w1"] = x["hy_f_w1"].transpose(1, 0, 2)
    arrays["f_w2"] = x["hy_f_w2"].transpose(1, 0, 2)
    arrays["f_w3"] = x["hy_f_w3"].transpose(1, 0, 2)
    arrays["f_col"] = np.stack([x["hy_f_b1"], x["hy_freq"][:, 0], x["hy_f_b2"], x["hy_freq"][:, 1]], -1).transpose(1, 0, 2)
    t = np.arange(SEQ)
    dr = t[None, :] // GRID_W - t[:, None] // GRID_W + 7
    dc = np.clip(t[None, :] % GRID_W - t[:, None] % GRID_W + 15, 0, 30)
    arrays["rpb"] = x["nat_rpb"][:, :, dr, dc].reshape(L, B_HEADS, 2, P, SEQ).transpose(0, 3, 2, 1, 4).reshape(L, P, 8 * SEQ)
    for n in ("ada_w", "ada_b", "w_in", "q_gain", "k_gain", "w_out", "ln1_g", "ln1_b", "ln2_g", "ln2_b", "router_w",
              "router_b", "exp_w1", "exp_w3", "exp_w2", "sh_w1", "sh_w3", "sh_w2"):
        arrays[n] = x[n]
    nc = bacc.Bacc("TRN2", target_bir_lowering=False, num_devices=1)
    feed, aps = {}, {}
    for n, v in arrays.items():
        v = np.ascontiguousarray(v)
        feed[f"in_{n}"] = v
        aps[n] = nc.dram_tensor(f"in_{n}", v.shape, mybir.dt.from_np(v.dtype), kind="ExternalInput").ap()
    out = nc.dram_tensor("out_latent", (SEQ, D), F32, kind="ExternalOutput").ap()
    scratch = (nc.dram_tensor("scratch_h", (TILES * P, D), F32).ap(),
               nc.dram_tensor("scratch_y", (TILES * P * TOP_K, D), F32).ap(),
               nc.dram_tensor("scratch_mod", (DEPTH, 2, 6 * D), F32).ap())
    hybrid_backbone(nc, aps, out, scratch)
    r = run_bass_kernel_spmd(nc, [feed], core_ids=[0])
    return r.results[0]["out_latent"].reshape(1, SEQ, D)
```
